# Optimizing a Trainium2 kernel written in Bass

```python
import jax, jax.numpy as jnp
from jax import lax
import numpy as np
import math

D_MODEL = 1024
BATCH = 1
SEQ = 256
DEPTH = 2

N_Q_HEADS = 16
N_KV_HEADS = 4
HEAD_DIM = 64
GROUP = N_Q_HEADS // N_KV_HEADS
WINDOW = 128
BLOCK = 128
ATTN_W = N_Q_HEADS * HEAD_DIM
KV_W = N_KV_HEADS * HEAD_DIM
CONV_W = D_MODEL
CONV_K = 3
REC_W = D_MODEL
REC_HEADS = 4
REC_HEAD_DIM = REC_W // REC_HEADS
REC_CONV_K = 4
LRU_C = 8.0
N_BRANCH = 3
BRANCH_W = D_MODEL
SPLIT_SIZES = (ATTN_W, KV_W, KV_W, CONV_W, CONV_W, CONV_W, REC_W, REC_W, N_BRANCH * D_MODEL)
IN_COLS = ATTN_W + 2 * KV_W + 3 * CONV_W + 2 * REC_W + N_BRANCH * D_MODEL
N_KEYS = 128
N_EXPERTS = N_KEYS * N_KEYS
PEER_HEADS = 8
PEER_TOPK = 16
PEER_KEY_DIM = 256
PEER_HALF = PEER_KEY_DIM // 2
PEER_CHUNK = 128
PLE_DIM = 256
EPS = 1e-6
NEG_INF = -1e30


def rmsnorm(x, g):
    x32 = x.astype(jnp.float32)
    y = x32 * lax.rsqrt(jnp.mean(x32 * x32, axis=-1, keepdims=True) + EPS) * g.astype(jnp.float32)
    return y.astype(x.dtype)

def causal_depthwise_conv(x, w, b=None):
    k_width, ch = w.shape
    y = lax.conv_general_dilated(
        x, w[:, None, :].astype(x.dtype), window_strides=(1,), padding=[(k_width - 1, 0)],
        dimension_numbers=('NWC', 'WIO', 'NWC'), feature_group_count=ch)
    if b is not None:
        y = y + b.astype(y.dtype)
    return y

def sliding_window_attention(q, k, v, sinks):
    b, s = q.shape[0], q.shape[1]
    nb = s // BLOCK
    qb = q.reshape(b, nb, BLOCK, N_KV_HEADS, GROUP, HEAD_DIM)

    def band(t):
        tp = jnp.pad(t, ((0, 0), (BLOCK, 0), (0, 0), (0, 0)))
        prev = tp[:, :s].reshape(b, nb, BLOCK, N_KV_HEADS, HEAD_DIM)
        cur = t.reshape(b, nb, BLOCK, N_KV_HEADS, HEAD_DIM)
        return jnp.concatenate([prev, cur], axis=2)

    kb, vb = band(k), band(v)
    scores = jnp.einsum('bnqhgd,bnkhd->bnhgqk', qb, kb,
                        preferred_element_type=jnp.float32) * (HEAD_DIM ** -0.5)
    q_pos = jnp.arange(nb)[:, None, None] * BLOCK + jnp.arange(BLOCK)[None, :, None]
    k_pos = jnp.arange(nb)[:, None, None] * BLOCK - BLOCK + jnp.arange(2 * BLOCK)[None, None, :]
    diff = q_pos - k_pos
    mask = (diff >= 0) & (diff < WINDOW) & (k_pos >= 0)
    scores = jnp.where(mask[None, :, None, None], scores, NEG_INF)
    sink = sinks.astype(jnp.float32).reshape(1, 1, N_KV_HEADS, GROUP, 1, 1)
    m = jnp.maximum(scores.max(axis=-1, keepdims=True), sink)
    e = jnp.exp(scores - m)
    probs = e / (e.sum(axis=-1, keepdims=True) + jnp.exp(sink - m))
    out = jnp.einsum('bnhgqk,bnkhd->bnqhgd', probs.astype(v.dtype), vb)
    return out.reshape(b, s, ATTN_W)

def rg_lru(x, w_r, b_r, w_i, b_i, lam):
    b, s, _ = x.shape
    x32 = x.astype(jnp.float32)
    xh = x32.reshape(b, s, REC_HEADS, REC_HEAD_DIM)
    r = jax.nn.sigmoid(jnp.einsum('bshi,hij->bshj', xh, w_r.astype(jnp.float32)).reshape(b, s, REC_W)
                       + b_r.astype(jnp.float32))
    i = jax.nn.sigmoid(jnp.einsum('bshi,hij->bshj', xh, w_i.astype(jnp.float32)).reshape(b, s, REC_W)
                       + b_i.astype(jnp.float32))
    log_a = -LRU_C * r * jax.nn.softplus(-lam.astype(jnp.float32))
    a = jnp.exp(log_a)
    inp = jnp.sqrt(-jnp.expm1(2.0 * log_a)) * (i * x32)

    def combine(left, right):
        a1, b1 = left
        a2, b2 = right
        return a1 * a2, a2 * b1 + b2

    _, h = lax.associative_scan(combine, (a, inp), axis=1)
    return h.astype(x.dtype)

def peer(xn, w_q, sub_keys, u, v):
    b, s, d = xn.shape
    t = b * s
    xt = xn.reshape(t, d)
    q = (xt @ w_q).astype(jnp.float32).reshape(t, PEER_HEADS, 2, PEER_HALF)
    sc = jnp.einsum('thpc,pnc->thpn', q, sub_keys.astype(jnp.float32))
    top_s, top_i = lax.top_k(sc, PEER_TOPK)
    cand = top_s[:, :, 0, :, None] + top_s[:, :, 1, None, :]
    best_s, best_c = lax.top_k(cand.reshape(t, PEER_HEADS, PEER_TOPK * PEER_TOPK), PEER_TOPK)
    i1 = jnp.take_along_axis(top_i[:, :, 0], best_c // PEER_TOPK, axis=-1)
    i2 = jnp.take_along_axis(top_i[:, :, 1], best_c % PEER_TOPK, axis=-1)
    expert = i1 * N_KEYS + i2
    gate = jax.nn.softmax(best_s, axis=-1)
    nc = t // PEER_CHUNK

    def chunk_fn(args):
        xc, ec, gc = args
        act = jax.nn.gelu(jnp.einsum('cd,chkd->chk', xc, u[ec]))
        return jnp.einsum('chk,chkd->cd', (gc * act).astype(xc.dtype), v[ec])

    out = lax.map(chunk_fn, (xt.reshape(nc, PEER_CHUNK, d),
                             expert.reshape(nc, PEER_CHUNK, PEER_HEADS, PEER_TOPK),
                             gate.reshape(nc, PEER_CHUNK, PEER_HEADS, PEER_TOPK)))
    return out.reshape(b, s, d)

def first_inputs(seed: int = 0) -> dict:
    key = jax.random.key(seed)
    ks = jax.random.split(key, 26)
    f32 = jnp.float32

    def nrm(k, shape, scale):
        return jax.random.normal(k, shape, f32) * scale

    a0 = jax.random.uniform(ks[12], (DEPTH, REC_W), f32, 0.9, 0.999) ** (1.0 / LRU_C)
    return {
        "x": nrm(ks[0], (BATCH, SEQ, D_MODEL), 1.0),
        "p": nrm(ks[1], (DEPTH, BATCH, SEQ, PLE_DIM), 1.0),
        "norm_mix": 1.0 + nrm(ks[2], (DEPTH, D_MODEL), 0.02),
        "w_in": nrm(ks[3], (DEPTH, D_MODEL, IN_COLS), D_MODEL ** -0.5),
        "attn_sinks": nrm(ks[4], (DEPTH, N_Q_HEADS), 0.5),
        "conv_w": nrm(ks[5], (DEPTH, CONV_K, CONV_W), CONV_K ** -0.5),
        "rec_conv_w": nrm(ks[6], (DEPTH, REC_CONV_K, REC_W), REC_CONV_K ** -0.5),
        "rec_conv_b": nrm(ks[7], (DEPTH, REC_W), 0.02),
        "w_rgate": nrm(ks[8], (DEPTH, REC_HEADS, REC_HEAD_DIM, REC_HEAD_DIM), REC_HEAD_DIM ** -0.5),
        "b_rgate": nrm(ks[9], (DEPTH, REC_W), 0.02),
        "w_igate": nrm(ks[10], (DEPTH, REC_HEADS, REC_HEAD_DIM, REC_HEAD_DIM), REC_HEAD_DIM ** -0.5),
        "b_igate": nrm(ks[11], (DEPTH, REC_W), 0.02),
        "lru_lambda": jnp.log(a0) - jnp.log1p(-a0),
        "w_branch": nrm(ks[13], (DEPTH, N_BRANCH, BRANCH_W, D_MODEL), BRANCH_W ** -0.5),
        "w_out": nrm(ks[14], (DEPTH, D_MODEL, D_MODEL), D_MODEL ** -0.5),
        "norm_ffn": 1.0 + nrm(ks[15], (DEPTH, D_MODEL), 0.02),
        "w_peer_q": nrm(ks[16], (DEPTH, D_MODEL, PEER_HEADS * PEER_KEY_DIM), D_MODEL ** -0.5),
        "peer_sub_keys": nrm(ks[17], (DEPTH, 2, N_KEYS, PEER_HALF), PEER_HALF ** -0.5),
        "peer_u": nrm(ks[18], (DEPTH, N_EXPERTS, D_MODEL), D_MODEL ** -0.5),
        "peer_v": nrm(ks[19], (DEPTH, N_EXPERTS, D_MODEL), (PEER_HEADS * PEER_TOPK) ** -0.5),
        "norm_ple": 1.0 + nrm(ks[20], (DEPTH, D_MODEL), 0.02),
        "w_ple_gate": nrm(ks[21], (DEPTH, D_MODEL, D_MODEL), D_MODEL ** -0.5),
        "w_ple_proj": nrm(ks[22], (DEPTH, PLE_DIM, D_MODEL), PLE_DIM ** -0.5),
        "norm_final": 1.0 + nrm(ks[23], (D_MODEL,), 0.02),
    }

def first_block(x, p, norm_mix, w_in, attn_sinks, conv_w, rec_conv_w, rec_conv_b, w_rgate, b_rgate,
              w_igate, b_igate, lru_lambda, w_branch, w_out, norm_ffn, w_peer_q, peer_sub_keys,
              peer_u, peer_v, norm_ple, w_ple_gate, w_ple_proj, norm_final):
    b, s, d = x.shape
    split_points = np.cumsum(SPLIT_SIZES)[:-1].tolist()
    h = x
    for l in range(DEPTH):
        xn = rmsnorm(h, norm_mix[l])
        z = xn @ w_in[l]
        q, k, v, c_b, c_c, c_x, r_x, r_y, gates = jnp.split(z, split_points, axis=-1)
        attn = sliding_window_attention(q.reshape(b, s, N_Q_HEADS, HEAD_DIM),
                                        k.reshape(b, s, N_KV_HEADS, HEAD_DIM),
                                        v.reshape(b, s, N_KV_HEADS, HEAD_DIM), attn_sinks[l])
        conv = c_b * causal_depthwise_conv(c_c * c_x, conv_w[l])
        rec = jax.nn.gelu(r_y) * rg_lru(causal_depthwise_conv(r_x, rec_conv_w[l], rec_conv_b[l]),
                                        w_rgate[l], b_rgate[l], w_igate[l], b_igate[l], lru_lambda[l])
        branches = jnp.stack([attn, conv, rec], axis=0)
        y = jnp.einsum('nbsw,nwd->nbsd', branches, w_branch[l])
        g = jax.nn.sigmoid(gates.reshape(b, s, N_BRANCH, d))
        merged = jnp.einsum('bsnd,nbsd->bsd', g, y)
        h = h + merged @ w_out[l]
        h = h + peer(rmsnorm(h, norm_ffn[l]), w_peer_q[l], peer_sub_keys[l], peer_u[l], peer_v[l])
        ple_gate = jax.nn.sigmoid(rmsnorm(h, norm_ple[l]) @ w_ple_gate[l])
        h = h + ple_gate * (p[l] @ w_ple_proj[l])
    return rmsnorm(h, norm_final)


GDN_HEADS = 8
GDN_DK = 128
GDN_DV = 128
GDN_QK = GDN_HEADS * GDN_DK
GDN_WIDTH = GDN_HEADS * GDN_DV
GDN_CONV_CH = 2 * GDN_QK + GDN_WIDTH
CONV_WIDTH = 5
CHUNK = 64
DIFF_HEADS = 8
DIFF_DH = 64
DIFF_DV = 2 * DIFF_DH
DIFF_QK = DIFF_HEADS * 2 * DIFF_DH
DIFF_WIDTH = DIFF_HEADS * DIFF_DV
Q_BLOCK = 128
ROPE_THETA = 500000.0
ROPE_DIM = DIFF_DH // 4

_SEG = (GDN_QK, GDN_QK, GDN_WIDTH, 4 * GDN_HEADS, GDN_WIDTH,
        DIFF_QK, DIFF_QK, DIFF_WIDTH, DIFF_WIDTH, D_MODEL, D_MODEL)
N_IN = sum(_SEG)
SPLIT_IDX = tuple(sum(_SEG[:i + 1]) for i in range(len(_SEG) - 1))


def rmsnorm_2(x, w):
    xf = x.astype(jnp.float32)
    y = xf * lax.rsqrt(jnp.mean(xf * xf, axis=-1, keepdims=True) + EPS)
    return y.astype(x.dtype) * w

def l2norm(x):
    return x * lax.rsqrt(jnp.sum(x * x, axis=-1, keepdims=True) + EPS)

def short_conv(x, w):
    pad = CONV_WIDTH // 2
    return lax.conv_general_dilated(
        x, w[:, None, :].astype(x.dtype), window_strides=(1,), padding=[(pad, pad)],
        dimension_numbers=("NWC", "WIO", "NWC"), feature_group_count=x.shape[-1])

def chunk_gated_delta(q, k, v, g, beta):
    f32 = jnp.float32
    q, k, v, g, beta = (t.astype(f32) for t in (q, k, v, g, beta))
    bsz, nh, seq, dk = k.shape
    dv = v.shape[-1]
    nc = seq // CHUNK
    q = q * dk ** -0.5
    kb = k * beta[..., None]
    vb = v * beta[..., None]
    rs = lambda t: t.reshape(bsz, nh, nc, CHUNK, t.shape[-1])
    q, k, kb, vb = rs(q), rs(k), rs(kb), rs(vb)
    g = jnp.cumsum(g.reshape(bsz, nh, nc, CHUNK), axis=-1)
    lower = jnp.tril(jnp.ones((CHUNK, CHUNK), dtype=bool))
    strict = jnp.tril(jnp.ones((CHUNK, CHUNK), dtype=bool), -1)
    gdiff = g[..., :, None] - g[..., None, :]
    decay = jnp.where(lower, jnp.exp(jnp.where(lower, gdiff, 0.0)), 0.0)
    L = jnp.where(strict, jnp.einsum('bhncd,bhnmd->bhncm', kb, k) * decay, 0.0)
    eye = jnp.eye(CHUNK, dtype=f32)
    T = lax.linalg.triangular_solve(eye + L, jnp.broadcast_to(eye, L.shape),
                                    left_side=True, lower=True, unit_diagonal=True)
    u = jnp.einsum('bhncm,bhnme->bhnce', T, vb)
    w = jnp.einsum('bhncm,bhnmd->bhncd', T, kb * jnp.exp(g)[..., None])
    qk = jnp.where(lower, jnp.einsum('bhncd,bhnmd->bhncm', q, k) * decay, 0.0)

    def step(state, inp):
        q_c, k_c, u_c, w_c, g_c, qk_c = inp
        v_new = u_c - jnp.einsum('bhcd,bhde->bhce', w_c, state)
        o = (jnp.einsum('bhcd,bhde->bhce', q_c * jnp.exp(g_c)[..., None], state)
             + jnp.einsum('bhcm,bhme->bhce', qk_c, v_new))
        g_last = g_c[..., -1]
        state = (state * jnp.exp(g_last)[..., None, None]
                 + jnp.einsum('bhcd,bhce->bhde', k_c * jnp.exp(g_last[..., None] - g_c)[..., None], v_new))
        return state, o

    xs = tuple(jnp.moveaxis(t, 2, 0) for t in (q, k, u, w, g, qk))
    state0 = jnp.zeros((bsz, nh, dk, dv), f32)
    _, o = lax.scan(step, state0, xs)
    return jnp.moveaxis(o, 0, 2).reshape(bsz, nh, seq, dv)

def gated_delta_branch(q, k, v, ab, z, conv_w, a_log, dt_bias, norm_w):
    bsz, seq, _ = q.shape
    f32 = jnp.float32
    qkv = jax.nn.silu(short_conv(jnp.concatenate([q, k, v], axis=-1), conv_w))
    q, k, v = jnp.split(qkv, (GDN_QK, 2 * GDN_QK), axis=-1)
    heads = lambda t, d: t.reshape(bsz, seq, GDN_HEADS, d).transpose(0, 2, 1, 3).astype(f32)
    q = l2norm(heads(q, GDN_DK))
    k = l2norm(heads(k, GDN_DK))
    v = heads(v, GDN_DV)
    ab = ab.reshape(bsz, seq, 4, GDN_HEADS).transpose(2, 0, 3, 1).astype(f32)
    beta = jax.nn.sigmoid(ab[:2])
    g = (-jnp.exp(a_log.astype(f32))[:, None, :, None]
         * jax.nn.softplus(ab[2:] + dt_bias.astype(f32)[:, None, :, None]))
    o_fwd = chunk_gated_delta(q, k, v, g[0], beta[0])
    flip = lambda t: jnp.flip(t, axis=2)
    o_bwd = flip(chunk_gated_delta(flip(q), flip(k), flip(v), flip(g[1]), flip(beta[1])))
    o = rmsnorm_2(o_fwd + o_bwd, norm_w.astype(f32))
    o = o.transpose(0, 2, 1, 3).reshape(bsz, seq, GDN_WIDTH).astype(z.dtype)
    return o * jax.nn.silu(z)

def partial_rope(t, cos, sin):
    half = ROPE_DIM // 2
    c = cos[:, :, None, None, :].astype(t.dtype)
    s = sin[:, :, None, None, :].astype(t.dtype)
    x1 = t[..., :half]
    x2 = t[..., half:ROPE_DIM]
    return jnp.concatenate([x1 * c - x2 * s, x2 * c + x1 * s, t[..., ROPE_DIM:]], axis=-1)

def diff_attention_branch(q, k, v, z, cos, sin, lam_params, subln_w, lambda_init):
    bsz, seq, _ = q.shape
    f32 = jnp.float32
    q = partial_rope(q.reshape(bsz, seq, DIFF_HEADS, 2, DIFF_DH), cos, sin) * (DIFF_DH ** -0.5)
    k = partial_rope(k.reshape(bsz, seq, DIFF_HEADS, 2, DIFF_DH), cos, sin)
    q = q.transpose(3, 0, 2, 1, 4)
    k = k.transpose(3, 0, 2, 1, 4)
    v = v.reshape(bsz, seq, DIFF_HEADS, DIFF_DV).transpose(0, 2, 1, 3)
    lp = lam_params.astype(f32)
    lam = jnp.exp(jnp.sum(lp[0] * lp[1])) - jnp.exp(jnp.sum(lp[2] * lp[3])) + lambda_init
    n_blk = seq // Q_BLOCK
    qb = q.reshape(2, bsz, DIFF_HEADS, n_blk, Q_BLOCK, DIFF_DH).transpose(3, 0, 1, 2, 4, 5)

    def attend(q_blk):
        s = jnp.einsum('nbhqd,nbhkd->nbhqk', q_blk, k).astype(f32)
        p = jax.nn.softmax(s, axis=-1)
        a = p[0] - lam * p[1]
        return jnp.einsum('bhqk,bhkd->bhqd', a.astype(v.dtype), v)

    o = lax.map(attend, qb)
    o = o.transpose(1, 2, 0, 3, 4).reshape(bsz, DIFF_HEADS, seq, DIFF_DV)
    o = rmsnorm_2(o, subln_w) * (1.0 - lambda_init)
    o = o.transpose(0, 2, 1, 3).reshape(bsz, seq, DIFF_WIDTH)
    return o * jax.nn.silu(z)

def second_inputs(seed: int = 0) -> dict:
    key = jax.random.key(seed)
    ks = jax.random.split(key, 16)
    f32 = jnp.float32
    x = jax.random.normal(ks[0], (BATCH, SEQ, D_MODEL), f32)
    positions = (jnp.arange(SEQ, dtype=jnp.int32)[None, :]
                 + jax.random.randint(ks[1], (BATCH, 1), 0, 4096, dtype=jnp.int32))
    norm_w = 1.0 + 0.02 * jax.random.normal(ks[2], (DEPTH, D_MODEL), f32)
    w_in = jax.random.normal(ks[3], (DEPTH, D_MODEL, N_IN), f32) * D_MODEL ** -0.5
    conv_w = jax.random.normal(ks[4], (DEPTH, CONV_WIDTH, GDN_CONV_CH), f32) * CONV_WIDTH ** -0.5
    a_log = jnp.log(jax.random.uniform(ks[5], (DEPTH, 2, GDN_HEADS), f32, 1.0, 16.0))
    dt = jnp.exp(jax.random.uniform(ks[6], (DEPTH, 2, GDN_HEADS), f32, math.log(1e-3), math.log(1e-1)))
    dt_bias = dt + jnp.log(-jnp.expm1(-dt))
    gdn_norm_w = 1.0 + 0.02 * jax.random.normal(ks[7], (DEPTH, GDN_DV), f32)
    diff_lambda = 0.1 * jax.random.normal(ks[8], (DEPTH, 4, DIFF_DH), f32)
    diff_subln_w = 1.0 + 0.02 * jax.random.normal(ks[9], (DEPTH, DIFF_DV), f32)
    w_pa = jax.random.normal(ks[10], (DEPTH, GDN_WIDTH, D_MODEL), f32) * GDN_WIDTH ** -0.5
    w_pb = jax.random.normal(ks[11], (DEPTH, DIFF_WIDTH, D_MODEL), f32) * DIFF_WIDTH ** -0.5
    w_out = jax.random.normal(ks[12], (DEPTH, D_MODEL, D_MODEL), f32) * D_MODEL ** -0.5
    final_norm_w = 1.0 + 0.02 * jax.random.normal(ks[13], (D_MODEL,), f32)
    return {"x": x, "positions": positions, "norm_w": norm_w, "w_in": w_in, "conv_w": conv_w,
            "a_log": a_log, "dt_bias": dt_bias, "gdn_norm_w": gdn_norm_w,
            "diff_lambda": diff_lambda, "diff_subln_w": diff_subln_w, "w_pa": w_pa,
            "w_pb": w_pb, "w_out": w_out, "final_norm_w": final_norm_w}

def second_block(x, positions, norm_w, w_in, conv_w, a_log, dt_bias, gdn_norm_w,
              diff_lambda, diff_subln_w, w_pa, w_pb, w_out, final_norm_w):
    inv_freq = ROPE_THETA ** (-(jnp.arange(0, ROPE_DIM, 2, dtype=jnp.float32) / ROPE_DIM))
    angles = positions.astype(jnp.float32)[..., None] * inv_freq
    cos, sin = jnp.cos(angles), jnp.sin(angles)
    for l in range(DEPTH):
        h = rmsnorm_2(x, norm_w[l])
        proj = h @ w_in[l]
        (q_a, k_a, v_a, ab_a, z_a, q_b, k_b, v_b, z_b,
         gate_a, gate_b) = jnp.split(proj, SPLIT_IDX, axis=-1)
        y_a = gated_delta_branch(q_a, k_a, v_a, ab_a, z_a, conv_w[l], a_log[l], dt_bias[l], gdn_norm_w[l])
        lambda_init = 0.8 - 0.6 * math.exp(-0.3 * l)
        y_b = diff_attention_branch(q_b, k_b, v_b, z_b, cos, sin, diff_lambda[l], diff_subln_w[l], lambda_init)
        merged = (jax.nn.sigmoid(gate_a) * (y_a @ w_pa[l])
                  + jax.nn.sigmoid(gate_b) * (y_b @ w_pb[l]))
        x = x + merged @ w_out[l]
    return rmsnorm_2(x, final_norm_w)


def setup_inputs(seed=0):
    out = dict(first_inputs(seed))
    for name, value in second_inputs(seed + 1).items():
        if name != "x":
            out[name + "_2"] = value
    return out


def reference(
    x, p, norm_mix, w_in, attn_sinks, conv_w, rec_conv_w, rec_conv_b, w_rgate, b_rgate, w_igate,
    b_igate, lru_lambda, w_branch, w_out, norm_ffn, w_peer_q, peer_sub_keys, peer_u, peer_v,
    norm_ple, w_ple_gate, w_ple_proj, norm_final, positions_2, norm_w_2, w_in_2, conv_w_2,
    a_log_2, dt_bias_2, gdn_norm_w_2, diff_lambda_2, diff_subln_w_2, w_pa_2, w_pb_2, w_out_2,
    final_norm_w_2,
):
    x = first_block(
        x, p, norm_mix, w_in, attn_sinks, conv_w, rec_conv_w, rec_conv_b, w_rgate, b_rgate,
        w_igate, b_igate, lru_lambda, w_branch, w_out, norm_ffn, w_peer_q, peer_sub_keys,
        peer_u, peer_v, norm_ple, w_ple_gate, w_ple_proj, norm_final,
    )
    return second_block(
        x, positions_2, norm_w_2, w_in_2, conv_w_2, a_log_2, dt_bias_2, gdn_norm_w_2,
        diff_lambda_2, diff_subln_w_2, w_pa_2, w_pb_2, w_out_2, final_norm_w_2,
    )


_drawn_inputs = setup_inputs


def setup_inputs(seed=0):
    import zlib

    import numpy as np

    out = dict(_drawn_inputs(seed))
    spreads = {}
    factors = {'attn_sinks': 6.594,
     'b_rgate': 8.0,
     'b_igate': 8.0,
     'norm_ffn': 5.917,
     'norm_ple': 8.0,
     'norm_w_2': 3.024,
     'gdn_norm_w_2': 6.975,
     'diff_subln_w_2': 8.0,
     'final_norm_w_2': 2.768}
    for name, (base, spread) in spreads.items():
        noise = np.random.default_rng([zlib.crc32(name.encode()), seed]).standard_normal(out[name].shape)
        drawn = base * np.exp(spread * noise) if base else spread * noise
        out[name] = __import__('jax').numpy.asarray(drawn.astype(out[name].dtype))
    for name, factor in factors.items():
        out[name] = (out[name] * factor).astype(out[name].dtype)
    return out
```

```python
from contextlib import contextmanager
from itertools import chain as chain_of, zip_longest

import numpy as np
import concourse.bass as bass
from concourse import mybir

F32 = mybir.dt.float32
I32 = mybir.dt.int32
U32 = mybir.dt.uint32
ALU = mybir.AluOpType
ACT = mybir.ActivationFunctionType
AX = mybir.AxisListType.X
ET = mybir.EngineType

P = 128
DEPTH = 2
SEQ = 256
NT = SEQ // P
D = 1024
KD = D // P
EPS = 1e-6
NEG = -1e30
BLK = 512
RING = 3

NQ, NKV, HD = 16, 4, 64
GRP = NQ // NKV
NKEYS = 128
NEXP = NKEYS * NKEYS
LRU_C = 8.0
DK, CHUNK = 128, 64
DHEADS, DH = 8, 64
ROPE, ROPE_THETA = DH // 4, 500000.0
C_AB, C_ZA, C_QB, C_KB, C_VB, C_ZB, C_GA, C_GB = 3072, 3104, 4128, 5152, 6176, 7200, 8224, 9248
PACE_INPUTS = ["pp"] * 4 + ["ppa"] * 8
PACE_FIRST = ["a", "apa"] * 13
PACE_SECOND = ["", "p"] * 13
BLK2 = 256
ROUND = float(3 * 2 ** 22)
TWO_PI = (6.28125, 0.0019350051879882812, 3.0199157e-07)
V1 = {}
_row = 0
for _name, _n in (("norm_mix", 8), ("conv_w", 24), ("rec_conv_w", 32), ("rec_conv_b", 8), ("b_rgate", 8),
                  ("b_igate", 8), ("lru_lambda", 8), ("norm_ffn", 8), ("norm_ple", 8)):
    V1[_name] = (_row, _n)
    _row += _n
NV1 = _row


class Clock:

    def __init__(self, nc, eng, name):
        self.eng, self.sem, self.n = eng, nc.alloc_semaphore(name), 0
        self.turn, self.per, self.loop = None, 0, None
        self.apart = None

    def done(self, ins):
        ins.then_inc(self.sem, 1)
        self.n += 1
        return Tick(self, self.n, self.loop)

    def after(self, *ticks):
        for t in ticks:
            if t is not None:
                t.wait(self.eng, self.apart)

    def link(self, ins):
        t = self.done(ins)
        self.after(t)
        return t


class Load:

    def __init__(self, nc, name):
        self.sem, self.n = nc.alloc_semaphore(name), 0
        self.turn, self.per, self.loop = None, 0, None

    def start(self, dma):
        dma.then_inc(self.sem, 16)
        self.n += 16
        return Tick(self, self.n, self.loop)


class Tick:
    def __init__(self, clock, n, loop):
        self.clock, self.n, self.loop = clock, n, loop

    def wait(self, eng, apart=None):
        c = self.clock
        if self.loop is not None and c.loop is self.loop:
            eng.wait_ge(c.sem, c.turn * c.per + self.n)
            if apart is not None:
                eng.sem_inc(apart)
            return
        n = self.n
        if self.loop is not None:
            n += (self.loop["turns"] - 1) * self.loop[c]
        eng.wait_ge(c.sem, n)


@contextmanager
def loop(nc, turns, engines, per):
    start = {c: c.n for c in per}
    with nc.Fori(0, turns, engines=engines) as i:
        rec = dict(per)
        rec["turns"] = turns
        for c in per:
            c.turn, c.per, c.loop = i, per[c], rec
        yield i
        made = {c.sem.name: c.n - start[c] for c in per}
        for c in per:
            assert c.n - start[c] == per[c], made
    for c in per:
        c.n = start[c] + turns * per[c]
        c.turn, c.per, c.loop = None, 0, None


def const_layout():
    at, n = {}, 0
    for name, w in CONSTANTS:
        at[name] = (n, w)
        n += w
    return at, n


CONSTANTS = [("ident", 128), ("mask_first", 128), ("mask_band", 256), ("iota16", 16), ("rope_turn", 128),
             ("inv_freq", 1), ("same_chunk", 128), ("chunk_0", 128), ("chunk_1", 128)]
CONSTANTS += [(f"{side}_{what}", 128) for side in ("low", "up") for what in ("incl", "far", 1, 2, 4, 8, 16, 32)]


def const_array():
    at, n = const_layout()
    c = np.zeros((P, n), np.float32)
    i, j = np.arange(P)[:, None], np.arange(P)[None, :]

    def put(name, v):
        c[:, at[name][0]:at[name][0] + at[name][1]] = v

    put("ident", i == j)
    put("mask_first", np.where(j <= i, 0.0, NEG))
    put("mask_band", np.concatenate([np.where(j > i, 0.0, NEG), np.where(j <= i, 0.0, NEG)], axis=1))
    put("iota16", np.arange(16)[None, :])
    half = ROPE // 2
    m, k = j, i
    d = m % DH
    put("rope_turn", np.where((d < half) & (k == m + half), -1.0, 0.0) + np.where((d >= half) & (d < ROPE) & (k == m - half), 1.0, 0.0))
    inv = (np.float32(ROPE_THETA) ** (-(np.arange(0, ROPE, 2, dtype=np.float32) / np.float32(ROPE)))).astype(np.float32)
    d = np.arange(P) % DH
    put("inv_freq", np.where(d < ROPE, inv[d % half], 0.0)[:, None])
    same = i // CHUNK == j // CHUNK
    put("same_chunk", same)
    put("chunk_0", i < CHUNK)
    put("chunk_1", i >= CHUNK)
    low = {"incl": same & (j <= i)}
    low["far"] = np.where(low["incl"], 0.0, 1e30)
    for s in (1, 2, 4, 8, 16, 32):
        low[s] = (i // (2 * s) == j // (2 * s)) & (i % (2 * s) >= s) & (j % (2 * s) < s)
    for what, v in low.items():
        put(f"low_{what}", v)
        put(f"up_{what}", v.T)
    return c


class Chip:

    def __init__(self, nc, consts):
        self.nc = nc
        self.first_sem = nc.alloc_semaphore("first_of_layer")
        self.T = Clock(nc, nc.tensor, "tensor_clock")
        self.A = Clock(nc, nc.scalar, "scalar_clock")
        self.V = Clock(nc, nc.vector, "vector_clock")
        self.G = Clock(nc, nc.gpsimd, "gpsimd_clock")
        self.w_loaded = [nc.alloc_semaphore(f"weights_loaded_{s}") for s in range(RING)]
        self.w_used = nc.alloc_semaphore("weight_blocks_used")
        self.small = Load(nc, "small_loads")
        self.late = Load(nc, "late_loads")
        self.store = Load(nc, "stores")
        self.u_rows = [Load(nc, f"u_rows_{s}") for s in range(8)]
        self.v_rows = [Load(nc, f"v_rows_{s}") for s in range(8)]
        self.apart = nc.alloc_semaphore("wait_apart")
        self.last_sem = nc.alloc_semaphore("last_of_layer")
        self.const_sem = nc.alloc_semaphore("constants_loaded")

        def sb(name, shape, dt=F32):
            return nc.alloc_sbuf_tensor(name, shape, dt)

        self.sb = sb
        self.h = sb("residual", [P, NT, D])
        self.xT = sb("normed_T", [P, KD, SEQ])
        self.xn = sb("normed", [P, NT, D])
        self.tmp = sb("scratch", [P, NT, D])
        self.z = sb("projections", [P, 80, SEQ])
        self.ring = sb("weights", [P, RING * KD * BLK])
        self.w = [self.ring[:, s * KD * BLK:(s + 1) * KD * BLK].rearrange("p (k c) -> p k c", k=KD) for s in range(RING)]
        self.extra = sb("small_of_block_1_or_outputs_of_2", [P, NT * D])
        self.arena = sb("arena", [P, 5120])
        self.small_f = sb("small_values", [P, 640])
        self.c = sb("constants_sb", [P, consts.shape[1]])
        self.vec = sb("channel_vectors", [P, 136])
        self.st = sb("statistics", [P, 64])
        self.idx_u = sb("topk_index", [P, 8, 16], U32)
        self.experts = sb("experts", [P, 2, 16], I32)
        self.ps = [nc.alloc_psum_tensor(f"bank_{b}", [P, 512], F32) for b in range(8)]
        at, _ = const_layout()
        self.const = {k: self.c[:, a:a + n] for k, (a, n) in at.items()}
        self.ident = self.const["ident"]
        nc.sync.dma_start(self.c[:], consts).then_inc(self.const_sem, 16)
        for e in (nc.tensor, nc.vector, nc.scalar, nc.gpsimd):
            e.wait_ge(self.const_sem, 16)

    def reset(self):
        nc = self.nc
        nc.all_engine_barrier()
        nc.gpsimd.dma_reset(range(self.first_sem.num, self.last_sem.num + 1))
        nc.gpsimd.sem_clear(range(self.first_sem.num, self.last_sem.num + 1))
        nc.all_engine_barrier()
        for c in (self.T, self.A, self.V, self.G, self.small, self.late, self.store, *self.u_rows, *self.v_rows):
            c.n = 0

    def weights_wait(self, b, turn=None, per=0):
        v = 16 * (b // RING + 1)
        if turn is not None:
            v = turn * (16 * per // RING) + v
        self.nc.tensor.wait_ge(self.w_loaded[b % RING], v)

    def load_block(self, b, src, dst=None):
        sp = self.nc.sync
        if b >= RING:
            sp.wait_ge(self.w_used, b - RING + 1)
        sp.dma_start(self.w[b % RING][:] if dst is None else dst, src).then_inc(self.w_loaded[b % RING], 16)

    def block_fm(self, slot, x, banks, after=None):
        T = self.T
        first = None
        for c in range(4):
            bank = banks[c // 2]
            if after is not None and c % 2 == 0:
                T.after(after[c // 2])
            for k in range(KD):
                m = self.nc.tensor.matmul(bank[:, (c % 2) * SEQ:(c % 2 + 1) * SEQ],
                                          lhsT=self.w[slot][:, k, c * P:(c + 1) * P], rhs=x[:, k, :],
                                          start=k == 0, stop=k == KD - 1)
            if c == 1:
                first = T.done(m)
        m.then_inc(self.w_used, 1)
        return first

    def block_tm(self, slot, x, banks, nk=KD, release=True, wview=None):
        w = self.w[slot] if wview is None else wview
        ticks = []
        for t in range(NT):
            for k in range(nk):
                m = self.nc.tensor.matmul(banks[t][:], lhsT=x[:, k, t * P:(t + 1) * P], rhs=w[:, k, :],
                                          start=k == 0, stop=k == nk - 1)
            if t == NT - 1 and release:
                m.then_inc(self.w_used, 1)
                ticks.append(None)
            else:
                ticks.append(self.T.done(m))
        return ticks

    def rms_scale(self, x, after):
        A, V, st = self.A, self.V, self.st
        squares = self.xT[:].rearrange("p k n -> p (k n)").rearrange("p (t c) -> p t c", t=NT)
        A.after(*after)
        V.after(*after)
        ss = A.done(self.nc.scalar.activation(squares[:, 0, :], x[:, 0, :], ACT.Square, accum_out=st[:, 0:1]))
        V.link(self.nc.vector.scalar_tensor_tensor(out=squares[:, 1, :], in0=x[:, 1, :], scalar=1.0, in1=x[:, 1, :],
                                                   op0=ALU.mult, op1=ALU.mult, accum_out=st[:, 1:2]))
        V.after(ss)
        A.after(V.done(self.nc.vector.tensor_scalar(st[:, 2:2 + NT], st[:, 0:NT], 1.0 / D, EPS, ALU.mult, ALU.add)))
        V.after(A.done(self.nc.scalar.activation(st[:, 6:6 + NT], st[:, 2:2 + NT], ACT.Sqrt)))
        V.link(self.nc.vector.reciprocal(st[:, 4:4 + NT], st[:, 6:6 + NT]))

    def norm_T(self, x, gain, after, vectors=None):
        nc, T, V = self.nc, self.T, self.V
        self.rms_scale(x, after)
        scaled = [V.done(nc.vector.tensor_scalar(self.xn[:, t, :], x[:, t, :], self.st[:, 4 + t:5 + t], None, ALU.mult))
                  for t in range(NT)]
        if vectors is not None:
            vectors()
        for t in range(NT):
            T.after(scaled[t])
            for q in range(2):
                for j in range(4):
                    m = nc.tensor.transpose(self.ps[2 * t + q][:, j * P:(j + 1) * P],
                                            self.xn[:, t, (4 * q + j) * P:(4 * q + j + 1) * P], self.ident)
                V.after(T.done(m))
                out = V.done(nc.vector.tensor_tensor(
                    self.xT[:, 4 * q:4 * q + 4, t * P:(t + 1) * P],
                    self.ps[2 * t + q][:].rearrange("p (j n) -> p j n", j=4),
                    gain[:, 4 * q:4 * q + 4].unsqueeze(2).to_broadcast([P, 4, P]), ALU.mult))
        return out

    def vectors(self, rows, n, dst):
        nc, T, V = self.nc, self.T, self.V
        T.after(*rows)
        t = T.done(nc.tensor.transpose(self.ps[5][:, 0:n], self.tmp[0:n, 0, 0:P], self.ident[0:n, 0:n]))
        V.after(t)
        return V.link(nc.vector.tensor_copy(dst, self.ps[5][:, 0:n]))


def softplus(chip, out, x, tmp):
    nc, V, A = chip.nc, chip.V, chip.A
    v = nc.vector
    u, s, q = tmp
    V.link(v.tensor_scalar(u, x, -1.0, None, ALU.mult))
    t = V.done(v.tensor_tensor(u, u, x, ALU.min))
    A.after(t)
    t = A.done(nc.scalar.activation(u, u, ACT.Exp))
    V.after(t)
    V.link(v.tensor_scalar(s, u, 2.0, None, ALU.add))
    V.link(v.reciprocal(s, s))
    V.link(v.tensor_tensor(s, s, u, ALU.mult))
    V.link(v.tensor_tensor(u, s, s, ALU.mult))
    V.link(v.tensor_scalar(q, u, 1.0 / 17, 1.0 / 15, ALU.mult, ALU.add))
    for n in (13, 11, 9, 7, 5, 3, 1):
        V.link(v.tensor_tensor(q, q, u, ALU.mult))
        V.link(v.tensor_scalar(q, q, 1.0 / n, None, ALU.add))
    V.link(v.tensor_tensor(q, q, s, ALU.mult))
    V.link(v.tensor_scalar(s, x, 0.0, None, ALU.max))
    return V.link(v.scalar_tensor_tensor(out=out, in0=q, scalar=2.0, in1=s, op0=ALU.mult, op1=ALU.add))


def conv_steps(chip, out, x, taps, w_of, tmp, shift_of):
    nc, V = chip.nc, chip.V
    n = out.shape[1]
    for k in sorted(range(taps), key=lambda k: shift_of(k) != 0):
        s = shift_of(k)
        a, b = max(0, -s), SEQ - max(0, s)
        w = w_of(k).unsqueeze(2).to_broadcast([P, n, b - a])
        src = x[:, :, a + s:b + s]
        if s == 0:
            V.link(nc.vector.tensor_tensor(out, src, w, ALU.mult))
        else:
            V.link(nc.vector.tensor_tensor(tmp[:, :, a:b], src, w, ALU.mult))
            V.link(nc.vector.tensor_tensor(out[:, :, a:b], out[:, :, a:b], tmp[:, :, a:b], ALU.add))
        yield


def block_one(chip, io):
    nc, T, A, V = chip.nc, chip.T, chip.A, chip.V
    v, act, ten, sp = nc.vector, nc.scalar, nc.tensor, nc.sync
    ps, z, st, h, xT, xn, tmp, ar = chip.ps, chip.z, chip.st, chip.h, chip.xT, chip.xn, chip.tmp, chip.arena
    ident = chip.ident

    ZQ, ZCB, ZCC, ZCX, ZRX, ZRY, ZG = 0, 8, 16, 24, 32, 40, 48
    kd = z[:, 72:76, :]
    e = chip.extra
    vt = e[:, 0:NT * NKV * HD].rearrange("p (t c) -> p t c", t=NT)
    sink, lru, layer_base = e[:, 512:512 + NQ], e[:, 528:536], e[:, 536:537]
    p_tok = e[:, 1024:1536].rearrange("p (t c) -> p t c", t=NT)
    pT = e[:, 1536:2048].rearrange("p (k n) -> p k n", k=2)
    pT_attn = [ar[:, n * 512:(n + 1) * 512] for n in range(2)]
    rec_x, gate_r = (ar[:, a:a + 2048].rearrange("p (k n) -> p k n", k=8) for a in (1024, 3072))
    projected = ar[:, 3072:5120].rearrange("p (t c) -> p t c", t=NT)

    def vec(name, k=0, n=8):
        a = V1[name][0] + 8 * k
        return chip.vec[:, a:a + n]

    V.link(v.memset(layer_base, 0.0))
    chip.reset()
    with nc.Fori(0, DEPTH) as l:
        for name in V1:
            a, n = V1[name]
            src = io[name][l]
            src = src.rearrange("(k p) -> k p", p=P) if len(src.shape) == 1 else src.rearrange("a (k p) -> (a k) p", p=P)
            staged = chip.small.start(sp.dma_start(tmp[a:a + n, 0, 0:P], src))
        chip.small.start(sp.dma_start(p_tok, io["p"][l, 0].rearrange("(t p) c -> p t c", p=P)))
        staged = chip.small.start(sp.dma_start(sink, io["attn_sinks"][bass.ds(l, 1), :].to_broadcast([P, NQ])))
        w_in = io["w_in"].rearrange("l (k p) c -> l p k c", p=P)
        b = 0
        block_of = {}
        for name, first, n in (("kv", D, 1), ("q", 0, 2), ("rx", 4608, 2), ("conv", 1536, 6)):
            block_of[name] = b
            for q in range(n):
                chip.load_block(b, w_in[l, :, :, first + q * BLK:first + (q + 1) * BLK])
                b += 1
        gates_src = [io["w_rgate"][l].rearrange("h (k p) c -> p h k c", p=P),
                     io["w_igate"][l].rearrange("h (k p) c -> p h k c", p=P)]
        w_gate_view = [chip.w[s].rearrange("p k c -> p (k c)")[:, 0:2048].rearrange("p (h k c) -> p h k c", h=4, k=2)
                       for s in range(RING)]
        block_of["lru_gates"] = b
        for g in range(2):
            chip.load_block(b, gates_src[g], w_gate_view[b % RING])
            b += 1
        for name, first, n in (("ry", 5632, 2), ("gates", 6656, 6)):
            block_of[name] = b
            for q in range(n):
                chip.load_block(b, w_in[l, :, :, first + q * BLK:first + (q + 1) * BLK])
                b += 1
        wb = io["w_branch"].rearrange("l n (k p) c -> l n p k c", p=P)
        wo = io["w_out"].rearrange("l (k p) c -> l p k c", p=P)
        wq = io["w_peer_q"].rearrange("l (k p) c -> l p k c", p=P)
        wg = io["w_ple_gate"].rearrange("l (k p) c -> l p k c", p=P)
        branch_order = (0, 1, 2)
        B_BRANCH = b
        for n in branch_order:
            for hlf in range(2):
                chip.load_block(b, wb[l, n, :, :, hlf * BLK:(hlf + 1) * BLK])
                b += 1
        for hlf in range(2):
            chip.load_block(b, wo[l, :, :, hlf * BLK:(hlf + 1) * BLK])
            b += 1
        B_PROJ = b
        proj_view = chip.w[b % RING].rearrange("p k c -> p (k c)")[:, 0:2048].rearrange("p (k c) -> p k c", k=2)
        chip.load_block(b, io["w_ple_proj"][l].rearrange("(k p) c -> p k c", p=P), proj_view)
        b += 1
        B_PQ = b
        for j in range(4):
            chip.load_block(b, wq[l, :, :, j * BLK:(j + 1) * BLK])
            b += 1
        B_PLE = b
        for hlf in range(2):
            chip.load_block(b, wg[l, :, :, hlf * BLK:(hlf + 1) * BLK])
            b += 1

        normed = chip.norm_T(h, vec("norm_mix"), [], lambda: chip.vectors([staged], NV1, chip.vec[:, 0:NV1]))
        for t in range(NT):
            for k in range(2):
                m = ten.transpose(ps[4][:, (k * NT + t) * P:(k * NT + t + 1) * P], p_tok[:, t, k * P:(k + 1) * P], ident)
        p_turned = T.done(m)
        A.after(p_turned)
        A.done(act.activation(pT, ps[4][:].rearrange("p (k n) -> p k n", k=2), ACT.Copy))
        neg = chip.sp_tmp[:, 0, 16:24]
        V.link(v.tensor_scalar(neg, vec("lru_lambda"), -1.0, None, ALU.mult))
        softplus(chip, lru, neg, [chip.sp_tmp[:, j, 0:8] for j in range(3)])

        T.after(normed)
        chip.weights_wait(0)
        for c in range(2):
            for k in range(KD):
                m = ten.matmul(ps[0][:, c * SEQ:(c + 1) * SEQ], lhsT=chip.w[0][:, k, c * P:(c + 1) * P],
                               rhs=xT[:, k, :], start=k == 0, stop=k == KD - 1)
        kt = T.done(m)
        for t in range(NT):
            for k in range(KD):
                m = ten.matmul(ps[1][:, t * 256:(t + 1) * 256], lhsT=xT[:, k, t * P:(t + 1) * P],
                               rhs=chip.w[0][:, k, 256:512], start=k == 0, stop=k == KD - 1)
        m.then_inc(chip.w_used, 1)
        A.after(kt)
        for j in range(NKV):
            src = ps[0][64 * (j % 2):64 * (j % 2) + 64, (j // 2) * SEQ:(j // 2 + 1) * SEQ]
            for half in range(2):
                kcopy = A.done(act.activation(kd[64 * half:64 * half + 64, j, :], src, ACT.Copy))
        act.wait_ge(chip.w_used, 1)
        vcopy = A.done(act.activation(vt.rearrange("p t c -> p (t c)"), ps[1][:], ACT.Copy))

        bank_read = {6: None, 7: None}

        def project(name, first_tile, fn=ACT.Copy):
            tile = first_tile
            for b in range(block_of[name], block_of[name] + {"kv": 1, "q": 2, "rx": 2, "conv": 6, "ry": 2, "gates": 6}[name]):
                chip.weights_wait(b)
                for u in range(2):
                    T.after(bank_read[6 + u])
                    for c in range(2):
                        for k in range(KD):
                            m = ten.matmul(ps[6 + u][:, c * SEQ:(c + 1) * SEQ],
                                           lhsT=chip.w[b % RING][:, k, (2 * u + c) * P:(2 * u + c + 1) * P], rhs=xT[:, k, :],
                                           start=k == 0, stop=k == KD - 1)
                        if c == 0:
                            yield
                    if u == 0:
                        A.after(T.done(m))
                    else:
                        m.then_inc(chip.w_used, 1)
                        act.wait_ge(chip.w_used, b + 1)
                    bank_read[6 + u] = A.done(act.activation(z[:, tile:tile + 2, :], ps[6 + u][:].rearrange("p (c n) -> p c n", c=2), fn))
                    tile += 2
                    yield

        scr = tmp[:].rearrange("p t d -> p (t d)").rearrange("p (k n) -> p k n", k=8)
        rx, ry = z[:, ZRX:ZRX + 8, :], z[:, ZRY:ZRY + 8, :]
        cb, cc, cx = z[:, ZCB:ZCB + 8, :], z[:, ZCC:ZCC + 8, :], z[:, ZCX:ZCX + 8, :]

        def lru_gates():
            for g, dst in enumerate((gate_r, rx)):
                b = block_of["lru_gates"] + g
                chip.weights_wait(b)
                for hh in range(4):
                    bank = ps[6 + hh % 2]
                    T.after(bank_read[6 + hh % 2])
                    for c in range(2):
                        for k in range(2):
                            m = ten.matmul(bank[:, c * SEQ:(c + 1) * SEQ],
                                           lhsT=w_gate_view[b % RING][:, hh, k, c * P:(c + 1) * P], rhs=rec_x[:, 2 * hh + k, :],
                                           start=k == 0, stop=k == 1)
                    if hh == 3:
                        m.then_inc(chip.w_used, 1)
                        act.wait_ge(chip.w_used, b + 1)
                    else:
                        A.after(T.done(m))
                    for c in range(2):
                        j = 2 * hh + c
                        t_ = A.done(act.activation(dst[:, j, :], bank[:, c * SEQ:(c + 1) * SEQ], ACT.Sigmoid,
                                                   bias=vec("b_rgate" if g == 0 else "b_igate")[:, j:j + 1]))
                    bank_read[6 + hh % 2] = t_
                    if hh % 2:
                        yield

        def lru_chain():
            r, gi, a = gate_r, rx, rec_x
            V.after(bank_read[6], bank_read[7])
            V.link(v.tensor_tensor(gi, gi, rec_x, ALU.mult))
            la = V.link(v.scalar_tensor_tensor(out=r, in0=r, scalar=-LRU_C,
                                               in1=lru.unsqueeze(2).to_broadcast([P, 8, SEQ]), op0=ALU.mult, op1=ALU.mult))
            yield
            yield
            A.after(la)
            A.done(act.activation(a, r, ACT.Exp))
            th = A.done(act.activation(scr, r, ACT.Tanh, scale=-1.0))
            yield
            V.after(th)
            V.link(v.tensor_tensor(r, a, a, ALU.mult))
            sq = V.link(v.scalar_tensor_tensor(out=scr, in0=r, scalar=1.0, in1=scr, op0=ALU.add, op1=ALU.mult))
            yield
            A.after(sq)
            root = A.done(act.activation(scr, scr, ACT.Sqrt))
            yield
            V.after(root)
            V.link(v.tensor_tensor(gi, gi, scr, ALU.mult))
            for j in range(8):
                sc_ = V.done(v.tensor_tensor_scan(r[:, j, :], a[:, j, :], gi[:, j, :], 0.0, ALU.mult, ALU.add))
                if j % 4 == 3:
                    yield
            V.after(sc_)

        x_ready = []
        branch_ready = {}

        def recurrent_conv():
            yield from conv_steps(chip, rec_x, rx, 4, lambda k: vec("rec_conv_w", k), scr, lambda k: k - 3)
            x_ready.append(V.link(v.tensor_tensor(rec_x, rec_x, vec("rec_conv_b").unsqueeze(2).to_broadcast([P, 8, SEQ]), ALU.add)))

        def gated_conv():
            V.link(v.tensor_tensor(cc, cc, cx, ALU.mult))
            yield from conv_steps(chip, cx, cc, 3, lambda k: vec("conv_w", k), scr, lambda k: k - 2)
            branch_ready[1] = V.link(v.tensor_tensor(cb, cb, cx, ALU.mult))

        def others():
            yield from project("rx", ZRX)
            V.after(bank_read[6], bank_read[7])
            steps = recurrent_conv()
            for _ in project("conv", ZCB):
                next(steps, None)
                yield
            T.after(x_ready[-1])
            A.after(x_ready[-1])
            V.after(bank_read[6], bank_read[7])
            yield from lru_gates()
            steps = chain_of(lru_chain(), gated_conv())
            for _ in project("ry", ZRY):
                next(steps, None)
                yield
            A.after(bank_read[6], bank_read[7])
            ry_ready = A.link(act.activation(ry, ry, ACT.Gelu_apprx_tanh))
            for _ in project("gates", ZG, ACT.Sigmoid):
                next(steps, None)
                yield
            for _ in steps:
                pass
            V.after(ry_ready)
            branch_ready[2] = V.link(v.tensor_tensor(ry, ry, gate_r, ALU.mult))

        scale = float(HD) ** -0.5
        probs = z[:, 76:80, :]
        mx, ss, es_ = st[:, 16:20], st[:, 24:28], st[:, 20:24]
        attn_tok = xn

        def attention():
            T.after(bank_read[6], bank_read[7], kcopy, vcopy)
            scores_read = turned = out_read = None
            for blk in range(NT):
                nk = P * (blk + 1)
                for g in range(NKV):
                    T.after(scores_read)
                    for j in range(GRP):
                        hq = GRP * g + j
                        lo = 64 * (hq % 2)
                        m = ten.matmul(ps[j % 2][:, (j // 2) * 256:(j // 2) * 256 + nk],
                                       lhsT=z[lo:lo + 64, ZQ + hq // 2, blk * P:(blk + 1) * P],
                                       rhs=kd[lo:lo + 64, g, 0:nk], start=True, stop=True)
                    V.after(T.done(m), turned)
                    yield
                    mask = chip.const["mask_first"] if blk == 0 else chip.const["mask_band"]
                    for u in range(2):
                        scores_read = V.done(v.scalar_tensor_tensor(
                            out=probs[:, u:GRP:2, 0:nk], in0=ps[u][:].rearrange("p (a n) -> p a n", a=2)[:, :, 0:nk],
                            scalar=scale, in1=mask.unsqueeze(1).to_broadcast([P, 2, nk]), op0=ALU.mult, op1=ALU.add))
                    V.after(scores_read)
                    V.link(v.tensor_reduce(mx, probs[:, :, 0:nk], AX, ALU.max))
                    V.link(v.tensor_tensor(mx, mx, sink[:, GRP * g:GRP * g + GRP], ALU.max))
                    V.link(v.tensor_tensor(es_, sink[:, GRP * g:GRP * g + GRP], mx, ALU.subtract))
                    A.after(V.link(v.tensor_scalar(mx, mx, -1.0, None, ALU.mult)))
                    for j in range(GRP):
                        ex = A.done(act.activation(probs[:, j, 0:nk], probs[:, j, 0:nk], ACT.Exp, bias=mx[:, j:j + 1],
                                                   accum_out=ss[:, j:j + 1]))
                    es = A.done(act.activation(es_, es_, ACT.Exp))
                    yield
                    V.after(es)
                    V.link(v.tensor_tensor(ss, ss, es_, ALU.add))
                    V.link(v.reciprocal(ss, ss))
                    T.after(ex)
                    for kt_ in range(blk + 1):
                        for j in range(GRP):
                            m = ten.transpose(ps[2 + kt_][:, j * P:(j + 1) * P], probs[:, j, kt_ * P:(kt_ + 1) * P], ident)
                        turned = T.done(m)
                        A.after(turned)
                        pc = A.done(act.activation(pT_attn[kt_], ps[2 + kt_][:], ACT.Copy))
                    yield
                    T.after(pc, out_read)
                    for j in range(GRP):
                        for kt_ in range(blk + 1):
                            m = ten.matmul(ps[4][:, j * 64:(j + 1) * 64], lhsT=pT_attn[kt_][:, j * P:(j + 1) * P],
                                           rhs=vt[:, kt_, g * HD:(g + 1) * HD], start=kt_ == 0, stop=kt_ == blk)
                    pv = T.done(m)
                    yield
                    V.after(pv)
                    out_read = V.done(v.tensor_tensor(
                        attn_tok[:, blk, g * 256:(g + 1) * 256].rearrange("p (j d) -> p j d", j=GRP),
                        ps[4][:, 0:256].rearrange("p (j d) -> p j d", j=GRP),
                        ss.unsqueeze(2).to_broadcast([P, GRP, HD]), ALU.mult))
                    V.after(out_read)
                T.after(out_read)
                for q in range(2):
                    for j in range(4):
                        m = ten.transpose(ps[2 + q][:, j * P:(j + 1) * P], attn_tok[:, blk, (4 * q + j) * P:(4 * q + j + 1) * P], ident)
                    A.after(T.done(m))
                    yield
                    branch_ready[0] = A.done(act.activation(z[:, ZQ + 4 * q:ZQ + 4 * q + 4, blk * P:(blk + 1) * P],
                                                            ps[2 + q][:].rearrange("p (j n) -> p j n", j=4), ACT.Copy))
                    T.after(branch_ready[0])

        for _ in project("q", ZQ):
            pass
        side = attention()
        for n, _ in enumerate(others()):
            if n % 9 % 2 == 0:
                next(side, None)
        for _ in side:
            pass

        xs = {0: z[:, ZQ:ZQ + 8, :], 1: cb, 2: ry}
        V.after(Tick(A, A.n, None))
        b = B_BRANCH
        used = []
        for n in branch_order:
            T.after(branch_ready[n])
            for hlf in range(2):
                banks = ps[0:2] if b % 2 else ps[2:4]
                chip.weights_wait(b)
                first = chip.block_fm(b % RING, xs[n], banks, after=used[-4:-2] if len(used) >= 4 else None)
                for u in range(2):
                    V.after(first) if u == 0 else v.wait_ge(chip.w_used, b + 1)
                    tile = 4 * hlf + 2 * u
                    g = z[:, ZG + 8 * n + tile:ZG + 8 * n + tile + 2, :]
                    y = banks[u][:].rearrange("p (c n) -> p c n", c=2)
                    if n == branch_order[0]:
                        t_ = V.done(v.tensor_tensor(cx[:, tile:tile + 2, :], g, y, ALU.mult))
                    else:
                        t_ = V.link(v.tensor_tensor(g, g, y, ALU.mult))
                        m_ = V.done(v.tensor_tensor(cx[:, tile:tile + 2, :], cx[:, tile:tile + 2, :], g, ALU.add))
                    used.append(t_)
                b += 1
        merged = m_
        T.after(merged)
        for hlf in range(2):
            chip.weights_wait(b)
            banks = ps[4 * hlf:4 * hlf + 2]
            ticks = chip.block_tm(b % RING, cx, banks)
            for t in range(NT):
                v.wait_ge(chip.w_used, b + 1) if ticks[t] is None else V.after(ticks[t])
                hs = h[:, t, hlf * BLK:(hlf + 1) * BLK]
                h_done = V.done(v.tensor_tensor(hs, hs, banks[t][:], ALU.add))
            b += 1

        chip.weights_wait(B_PROJ)
        for hlf in range(2):
            banks = ps[2 + 4 * hlf:4 + 4 * hlf]
            ticks = chip.block_tm(B_PROJ % RING, pT, banks, nk=2, release=hlf == 1, wview=proj_view[:, :, hlf * BLK:(hlf + 1) * BLK])
            for t in range(NT):
                act.wait_ge(chip.w_used, B_PROJ + 1) if ticks[t] is None else A.after(ticks[t])
                p_done = A.done(act.activation(projected[:, t, hlf * BLK:(hlf + 1) * BLK], banks[t][:], ACT.Copy))
        T.after(p_done)
        peer(chip, io, l, h_done, B_PQ, vec, layer_base)

        n2 = chip.norm_T(h, vec("norm_ple"), [Tick(V, V.n, None)])
        T.after(n2)
        for hlf in range(2):
            b = B_PLE + hlf
            cs = slice(hlf * BLK, (hlf + 1) * BLK)
            chip.weights_wait(b)
            ticks = chip.block_tm(b % RING, xT, ps[2 * hlf:2 * hlf + 2])
            for t in range(NT):
                act.wait_ge(chip.w_used, b + 1) if ticks[t] is None else A.after(ticks[t])
                V.after(A.done(act.activation(tmp[:, t, cs], ps[2 * hlf + t][:], ACT.Sigmoid)))
                V.link(v.tensor_tensor(tmp[:, t, cs], tmp[:, t, cs], projected[:, t, cs], ALU.mult))
                V.link(v.tensor_tensor(h[:, t, cs], h[:, t, cs], tmp[:, t, cs], ALU.add))
        V.link(v.tensor_scalar(layer_base, layer_base, float(NEXP), None, ALU.add))
        chip.reset()


def peer(chip, io, l, h_done, b0, vec, layer_base):
    nc, T, A, V, G = chip.nc, chip.T, chip.A, chip.V, chip.G
    v, act, ten, pool, sp = nc.vector, nc.scalar, nc.tensor, nc.gpsimd, nc.sync
    ps, z, st, h, xT, xn, tmp = chip.ps, chip.z, chip.st, chip.h, chip.xT, chip.xn, chip.tmp
    ident = chip.ident
    ar, at = chip.arena, 0
    mem = {}
    for name, shape in (("keysT", (2, P)), ("cur", (2, 2, P)), ("cand", (2, 256)), ("hot", (2, 256)), ("coef", (2, 16)),
                        ("dots", (2, 16)), ("diag", (4, P)), ("small", (24, 16))):
        n = int(np.prod(shape))
        names = " ".join("abc"[:len(shape)])
        mem[name] = ar[:, at:at + n].rearrange(f"p ({names}) -> p {names}", **dict(zip("abc", shape)))
        at += n
    mem["idx_u"], mem["experts"] = chip.idx_u, chip.experts
    keysT, cur, sm, iu = mem["keysT"], mem["cur"], mem["small"], mem["idx_u"]
    zf = z[:].rearrange("p a n -> p (a n)")
    u_ring = [zf[:, s * D:(s + 1) * D] for s in range(8)]
    v_ring = [zf[:, (8 + s) * D:(9 + s) * D] for s in range(8)]
    scores = zf[:, 16 * D:20 * D].rearrange("p (i c) -> p i c", c=256)
    qT = tmp[:].rearrange("p t d -> p (t d)").rearrange("p (k n) -> p k n", k=8)

    pool.wait_ge(V.sem, h_done.n)
    keys_raw = z[:, 32, :].rearrange("p (a c) -> p a c", a=2)
    kin = chip.late.start(pool.dma_start(keys_raw, io["peer_sub_keys"][l].rearrange("a n c -> n a c")))
    gain_row = z[:, 36:40, :].rearrange("p a n -> p (a n)")
    kin = chip.late.start(pool.dma_start(gain_row, io["norm_ffn"][bass.ds(l, 1), :].to_broadcast([P, D])))
    normed = chip.norm_T(h, vec("norm_ffn"), [h_done])
    T.after(kin)
    for a in range(2):
        m = ten.transpose(ps[7][:, a * P:(a + 1) * P], keys_raw[:, a, :], ident)
    m = T.done(m)
    V.after(m, kin)
    keys_ready = V.link(v.tensor_copy(keysT[:].rearrange("p a n -> p (a n)"), ps[7][:, 0:2 * P]))

    iota = chip.const["iota16"]
    BIG = -3.0e38

    def fetch(buf, item):
        return A.done(act.activation(cur[:, buf, :, :].rearrange("p a n -> p (a n)"),
                                     scores[:, item, :] if isinstance(item, int) else
                                     scores[:, bass.ds(item, 1), :].rearrange("p i c -> p (i c)"), ACT.Copy))

    def top16(src, vals, idx):
        V.link(v.max(vals[:, 0:8], src))
        V.done(v.max_index(idx[:, 0:8], vals[:, 0:8], src))
        V.link(v.match_replace(src, vals[:, 0:8], src, BIG))
        V.link(v.max(vals[:, 8:16], src))
        return V.link(v.max_index(idx[:, 8:16], vals[:, 8:16], src))

    SEL = 31

    def select(buf):
        n0 = V.n
        V.apart = None if V.loop is None else chip.apart
        s_ = sm[:, 12 * buf:12 * buf + 12, :]
        tops = [s_[:, 0, :], s_[:, 1, :]]
        for a in range(2):
            top16(cur[:, buf, a, :], tops[a], iu[:, a, :])
        for a in range(2):
            V.done(v.tensor_copy(s_[:, 2 + a, :], iu[:, a, :]))
        cand = mem["cand"][:, buf, :]
        c3 = cand.rearrange("p (a b) -> p a b", a=16)
        V.link(v.tensor_tensor(c3, tops[0].unsqueeze(2).to_broadcast([P, 16, 16]),
                               tops[1].unsqueeze(1).to_broadcast([P, 16, 16]), ALU.add))
        best = s_[:, 4, :]
        top16(cand, best, iu[:, 2, :])
        V.done(v.tensor_scalar(iu[:, 3, :], iu[:, 2, :], 4, None, ALU.logical_shift_right))
        V.link(v.tensor_scalar(iu[:, 4, :], iu[:, 2, :], 15, None, ALU.bitwise_and))
        for a in range(2):
            V.link(v.tensor_copy(s_[:, 5 + a, :], iu[:, 3 + a, :]))
        hot = mem["hot"]
        for a in range(2):
            h3 = hot[:, a, :].rearrange("p (k j) -> p k j", k=16)
            V.link(v.tensor_tensor(h3, s_[:, 5 + a, :].unsqueeze(2).to_broadcast([P, 16, 16]),
                                   iota.unsqueeze(1).to_broadcast([P, 16, 16]), ALU.is_equal))
            V.link(v.tensor_tensor(h3, h3, s_[:, 2 + a, :].unsqueeze(1).to_broadcast([P, 16, 16]), ALU.mult))
            V.link(v.tensor_reduce(s_[:, 7 + a, :], h3, AX, ALU.add))
        V.link(v.scalar_tensor_tensor(out=s_[:, 7, :], in0=s_[:, 7, :], scalar=float(NKEYS), in1=s_[:, 8, :],
                                      op0=ALU.mult, op1=ALU.add))
        V.done(v.tensor_scalar(s_[:, 9, :], best, best[:, 0:1], None, ALU.subtract))
        e = V.link(v.tensor_scalar(mem["experts"][:, buf, :], s_[:, 7, :], layer_base[:, 0:1], None, ALU.add))
        V.apart = None
        assert V.n - n0 == SEL, V.n - n0
        return e

    T.after(normed, keys_ready)
    A.after(normed)
    copied, score_read = [], None

    def queries(j):
        b = b0 + j
        chip.weights_wait(b)
        banks = ps[2 * (j % 2):2 * (j % 2) + 2]
        first = chip.block_fm(b % RING, xT, banks, after=None if j < 2 else copied[j - 2])
        two = []
        for u in range(2):
            A.after(first) if u == 0 else act.wait_ge(chip.w_used, b + 1)
            q0 = 4 * (j % 2) + 2 * u
            two.append(A.done(act.activation(qT[:, q0:q0 + 2, :], banks[u][:].rearrange("p (c n) -> p c n", c=2), ACT.Copy)))
        copied.append(two)

    def score(j, t):
        nonlocal score_read
        T.after(copied[j][1], score_read)
        for c in range(4):
            m = ten.matmul(ps[4 + t][:, c * P:(c + 1) * P], lhsT=qT[:, 4 * (j % 2) + c, t * P:(t + 1) * P],
                           rhs=keysT[:, c % 2, :], start=True, stop=True)
        A.after(T.done(m))
        i0 = t * 8 + 2 * j
        score_read = A.link(act.activation(scores[:, i0:i0 + 2, :], ps[4 + t][:].rearrange("p (i c) -> p i c", i=2), ACT.Copy))

    for t in range(NT):
        V.link(v.tensor_tensor(xn[:, t, :], xn[:, t, :], gain_row, ALU.mult))
    for c in range(2):
        V.link(v.memset(ps[6 + c][:], 0.0))
    queries(0)
    score(0, 0)
    V.after(fetch(0, 0))
    select(0)
    score(0, 1)
    for j in range(1, 4):
        queries(j)
        if j > 1:
            score(j - 1, 0)
            score(j - 1, 1)
    score(3, 0)
    score(3, 1)
    uf = io["peer_u"].rearrange("l e d -> (l e) d")
    vf = io["peer_v"].rearrange("l e d -> (l e) d")
    HALF_V = 16 + 3 + 1 + SEL
    HALF_A = 1 + 2 + 16
    HALF_T = 16
    U_N, V_N, DG_N = len(u_ring), len(v_ring), 4
    per = {V: 2 * HALF_V, A: 2 * HALF_A, T: 2 * HALF_T}
    for q in range(8):
        per[chip.u_rows[q]] = per[chip.v_rows[q]] = 16 * 4
    v0, a0, t0 = V.n, A.n, T.n
    assert v0 > HALF_V and a0 > 2 * HALF_A and t0 > HALF_T, (v0, a0, t0)
    pool.wait_ge(V.sem, v0)
    with loop(nc, 8, [ET.PE, ET.Activation, ET.DVE, ET.Pool], per) as i:
        L = V.loop
        tile = i // 4
        for half in range(2):
            hv, ht = v0 + half * HALF_V, t0 + half * HALF_T
            ex = mem["experts"][:, half, :]
            Tick(V, hv, L).wait(pool, chip.apart)
            rows_u, rows_v = [], []
            for k in range(16):
                Tick(V, hv + k - U_N + 1 if k >= U_N else hv - HALF_V + 16 + k - U_N + 1, L).wait(pool, chip.apart)
                rows_u.append(chip.u_rows[k % U_N].start(pool.indirect_dma_start(
                    u_ring[k % U_N], None, uf, bass.IndirectOffsetOnAxis(ap=ex[:, k:k + 1], axis=0))))
            for k in range(16):
                Tick(T, ht + k - V_N + 1 if k >= V_N else ht - HALF_T + 16 + k - V_N + 1, L).wait(pool, chip.apart)
                rows_v.append(chip.v_rows[k % V_N].start(pool.indirect_dma_start(
                    v_ring[k % V_N], None, vf, bass.IndirectOffsetOnAxis(ap=ex[:, k:k + 1], axis=0))))
            nxt = i * 2 + 1 if half == 0 else (i * 2 + 2) % 16
            Tick(V, hv - HALF_V, L).wait(act, chip.apart)
            f = fetch(1 - half, nxt)
            dots = mem["dots"][:, half, :]
            for k in range(16):
                V.after(rows_u[k])
                d = V.done(v.scalar_tensor_tensor(
                    out=u_ring[k % U_N], in0=u_ring[k % U_N], scalar=1.0,
                    in1=xn[:, bass.ds(tile, 1), :].rearrange("p t d -> p (t d)"), op0=ALU.mult, op1=ALU.mult,
                    accum_out=dots[:, k:k + 1]))
            A.after(d)
            geluv, expv = sm[:, 12 * half + 10, :], sm[:, 12 * half + 11, :]
            A.done(act.activation(geluv, dots, ACT.Gelu_apprx_tanh))
            eg = A.done(act.activation(expv, sm[:, 12 * half + 9, :], ACT.Exp, accum_out=st[:, 40 + half:41 + half]))
            V.after(eg)
            V.link(v.reciprocal(st[:, 42 + half:43 + half], st[:, 40 + half:41 + half]))
            V.link(v.tensor_scalar(expv, expv, st[:, 42 + half:43 + half], None, ALU.mult))
            co = V.link(v.tensor_tensor(mem["coef"][:, half, :], geluv, expv, ALU.mult))
            banks = ps[4 + 2 * half:6 + 2 * half]
            A.after(co)
            Tick(V, hv, L).wait(ten)
            for k in range(16):
                Tick(T, ht + k - DG_N + 1, L).wait(act)
                dg = A.done(act.activation(mem["diag"][:, k % DG_N, :], ident, ACT.Copy,
                                           scale=mem["coef"][:, half, k:k + 1]))
                T.after(dg, rows_v[k])
                for c in range(2):
                    m = ten.matmul(banks[c][:], lhsT=mem["diag"][:, k % DG_N, :],
                                   rhs=v_ring[k % V_N][:, c * 512:(c + 1) * 512], start=k == 0, stop=k == 15)
                T.done(m)
            prev = (i * 2 + 15) % 16 // 8 if half == 0 else tile
            Tick(T, ht, L).wait(v)
            for c in range(2):
                hs = h[:, bass.ds(prev, 1), c * 512:(c + 1) * 512].rearrange("p t d -> p (t d)")
                ins = v.tensor_tensor(hs, hs, ps[4 + 2 * (1 - half) + c][:], ALU.add)
            V.done(ins)
            V.apart = chip.apart
            V.after(f)
            select(1 - half)
    V.after(Tick(T, T.n, None))
    for c in range(2):
        hs = h[:, 1, c * 512:(c + 1) * 512]
        V.link(v.tensor_tensor(hs, hs, ps[6 + c][:], ALU.add))


def final_norm(chip, out, gain_row_src):
    nc, V = chip.nc, chip.V
    row = chip.z[:, 0:4, :].rearrange("p a n -> p (a n)")
    g = chip.late.start(nc.sync.dma_start(row, gain_row_src.unsqueeze(0).to_broadcast([P, D])))
    chip.rms_scale(chip.h, [])
    V.after(g)
    for t in range(NT):
        done = V.link(nc.vector.scalar_tensor_tensor(out=out[:, t, :], in0=chip.h[:, t, :], scalar=chip.st[:, 4 + t:5 + t],
                                                     in1=row, op0=ALU.mult, op1=ALU.mult))
    return done


def rope_tables(chip, loaded, cos, sin):
    nc, V, A = chip.nc, chip.V, chip.A
    v = nc.vector
    w = chip.arena[:, 1024:2048]
    angle, turns = w[:, 0:SEQ], w[:, SEQ:2 * SEQ]
    pos = w[:, 3 * SEQ:4 * SEQ].bitcast(I32)
    V.after(loaded)
    V.link(v.tensor_copy(angle, pos))
    V.link(v.tensor_scalar(angle, angle, chip.const["inv_freq"], None, ALU.mult))
    for out, quarter in ((sin, 0.0), (cos, float(np.pi / 2))):
        V.link(v.tensor_scalar(turns, angle, quarter, 1.0 / (2 * np.pi), ALU.add, ALU.mult))
        V.link(v.tensor_scalar(turns, turns, ROUND, None, ALU.add))
        V.link(v.tensor_scalar(turns, turns, -ROUND, None, ALU.add))
        V.link(v.scalar_tensor_tensor(out=out, in0=turns, scalar=-TWO_PI[0], in1=angle, op0=ALU.mult, op1=ALU.add))
        for part in TWO_PI[1:]:
            V.link(v.scalar_tensor_tensor(out=out, in0=turns, scalar=-part, in1=out, op0=ALU.mult, op1=ALU.add))
        if quarter:
            V.link(v.tensor_scalar(out, out, quarter, None, ALU.add))
        r = V.link(v.tensor_scalar(out, out, -3.1415925, 3.1415925, ALU.max, ALU.min))
        A.after(r)
        A.done(nc.scalar.activation(out, out, ACT.Sin))
    return Tick(A, A.n, None)


def block_two(chip, io, rope):
    nc, T, A, V, G = chip.nc, chip.T, chip.A, chip.V, chip.G
    v, act, ten, pool, sp = nc.vector, nc.scalar, nc.tensor, nc.gpsimd, nc.sync
    ps, z, st, h, xT, xn, tmp = chip.ps, chip.z, chip.st, chip.h, chip.xT, chip.xn, chip.tmp
    ident, const = chip.ident, chip.const
    cos, sin = rope
    sf, ar = chip.small_f, chip.arena

    def tokens(flat):
        return flat.rearrange("p (t c) -> p t c", t=NT)

    def heads(x):
        return x.rearrange("p (h n) -> p h n", n=P)

    def tiles(a, n=8):
        return z[:, a:a + n, :]

    def flat(a):
        return z[:, a:a + 8, :].rearrange("p a n -> p (a n)")

    QA, KA, VA, ZA, QB, KB, ZB, GA, GB, VB = 0, 8, 16, 24, 32, 40, 48, 56, 64, 72
    vb = tokens(flat(VB))
    WB = KD * BLK2
    w2 = [chip.ring[:, s * WB:(s + 1) * WB].rearrange("p (k c) -> p k c", k=KD) for s in range(RING)]
    k_tok, QK, pflat = (chip.ring[:, n * WB:(n + 1) * WB] for n in range(3, 6))
    k_tok, O = tokens(k_tok), tokens(chip.extra[:])
    v_tok, q_tok = xn, tmp
    U_, w_T, QK = (tokens(flat(VA)), vb), (tmp, tokens(flat(QB))), (tokens(QK), tokens(pflat))

    def load(b, src):
        if b >= RING:
            sp.wait_ge(chip.w_used, b - RING + 1)
        sp.dma_start(w2[b % RING], src).then_inc(chip.w_loaded[b % RING], 16)

    chip.reset()
    with nc.Fori(0, DEPTH) as l:
        def vrow(x):
            return x.rearrange("(k p) -> k p", p=P)

        chip.small.start(sp.dma_start(tmp[0:8, 0, 0:P], vrow(io["norm_w_2"][l])))
        chip.small.start(sp.dma_start(tmp[8:128, 0, 0:P], io["conv_w_2"][l].rearrange("a (k p) -> (a k) p", p=P)))
        chip.small.start(sp.dma_start(tmp[0:1, 1, 0:P], io["gdn_norm_w_2"][bass.ds(l, 1), :]))
        chip.small.start(sp.dma_start(tmp[1:2, 1, 0:P], io["diff_subln_w_2"][bass.ds(l, 1), :]))
        rows = {"a_log_2": sf[:, 0:16], "dt_bias_2": sf[:, 16:32], "diff_lambda_2": ar[:, 0:256], "lambda_init": sf[:, 32:33]}
        for name, dst in rows.items():
            src = io[name]
            if len(src.shape) == 3:
                src = src.rearrange("l a b -> l (a b)")
            staged = chip.small.start(sp.dma_start(dst, src[bass.ds(l, 1), :].to_broadcast([P, dst.shape[1]])))
        staged = chip.small.start(sp.dma_start(ar[:, 1024 + 3 * SEQ:1024 + 4 * SEQ].bitcast(I32), io["positions_2"].to_broadcast([P, SEQ])))
        w_in = io["w_in_2"].rearrange("l (k p) c -> l p k c", p=P)
        wab = ar[:, 256:512].rearrange("p (k c) -> p k c", k=KD)
        ab_loaded = chip.late.start(sp.dma_start(wab, w_in[l, :, :, C_AB:C_AB + 32]))
        for b in range(RING):
            load(b, w_in[l, :, :, b * BLK2:(b + 1) * BLK2])
        with nc.sync.Fori(0, 3) as i:
            for s in range(RING):
                sp.wait_ge(chip.w_used, i * RING + (s + 1))
                sp.dma_start(w2[s], w_in[l, :, :, bass.ds(i * (RING * BLK2) + (RING + s) * BLK2, BLK2)])\
                  .then_inc(chip.w_loaded[s], 16)
        b = 12
        block_of = {}
        for name, col in (("qb", C_QB), ("kb", C_KB), ("vb", C_VB), ("zb", C_ZB), ("za", C_ZA), ("ga", C_GA), ("gb", C_GB)):
            block_of[name] = b
            for q in range(4):
                load(b, w_in[l, :, :, col + q * BLK2:col + (q + 1) * BLK2])
                b += 1
        for name in ("w_pb_2", "w_pa_2", "w_out_2"):
            block_of[name] = b
            wsrc = io[name].rearrange("l (k p) c -> l p k c", p=P)
            for q in range(4):
                load(b, wsrc[l, :, :, q * BLK2:(q + 1) * BLK2])
                b += 1

        zeroed = G.done(pool.memset(chip.extra[:], 0.0))
        normed = chip.norm_T(h, chip.vec[:, 0:8], [], lambda: chip.vectors([staged], 128, chip.vec[:, 0:128]))
        T.after(normed)
        T.after(ab_loaded)
        V.after(ab_loaded)
        for t in range(NT):
            for k in range(KD):
                m = ten.matmul(ps[4][:, t * 32:(t + 1) * 32], lhsT=xT[:, k, t * P:(t + 1) * P], rhs=wab[:, k, :],
                               start=k == 0, stop=k == KD - 1)
        ab_ready = T.done(m)
        T.after(Tick(V, V.n, None))
        t_ = T.done(ten.transpose(ps[1][:, 0:2], tmp[0:2, 1, 0:P], ident[0:2, 0:2]))
        V.after(t_)
        V.link(v.tensor_copy(chip.vec[:, 128:130], ps[1][:, 0:2]))
        nea, dt, linit = sf[:, 0:16], sf[:, 16:32], sf[:, 32:33]
        lam, subl = sf[:, 33:34], sf[:, 34:35]
        lv = ar[:, 0:256]
        for a in range(2):
            V.link(v.tensor_tensor(lv[:, a * 128:a * 128 + 64], lv[:, a * 128:a * 128 + 64], lv[:, a * 128 + 64:a * 128 + 128], ALU.mult))
            t_ = V.link(v.tensor_reduce(sf[:, 36 + a:37 + a], lv[:, a * 128:a * 128 + 64], AX, ALU.add))
        A.after(t_)
        A.done(act.activation(sf[:, 36:38], sf[:, 36:38], ACT.Exp))
        t_ = A.done(act.activation(nea, nea, ACT.Exp))
        V.after(t_)
        V.link(v.tensor_scalar(nea, nea, -1.0, None, ALU.mult))
        V.link(v.tensor_tensor(lam, sf[:, 36:37], sf[:, 37:38], ALU.subtract))
        V.link(v.tensor_tensor(lam, lam, linit, ALU.add))
        V.link(v.tensor_scalar(subl, linit, -1.0, 1.0, ALU.mult, ALU.add))
        V.link(v.tensor_tensor(subl, subl, chip.vec[:, 129:130], ALU.mult))

        rope_tables(chip, staged, cos, sin)
        with loop(nc, 4, [ET.PE, ET.Activation], {A: RING}) as i:
            for s in range(RING):
                bank = ps[5 + s]
                chip.weights_wait(s, i, RING)
                T.after(Tick(A, A.n + 1 - RING, A.loop))
                for c in range(2):
                    for k in range(KD):
                        m = ten.matmul(bank[:, c * SEQ:(c + 1) * SEQ], lhsT=w2[s][:, k, c * P:(c + 1) * P], rhs=xT[:, k, :],
                                       start=k == 0, stop=k == KD - 1)
                m.then_inc(chip.w_used, 1)
                act.wait_ge(chip.w_used, i * RING + (s + 1))
                act.sem_inc(chip.apart)
                A.done(act.activation(z[:, bass.ds(i * (2 * RING) + 2 * s, 2), :], bank[:].rearrange("p (c n) -> p c n", c=2), ACT.Copy))
        evacs = A.n
        bank_read = {6: Tick(A, evacs - 1, None), 7: Tick(A, evacs, None)}

        scr = tmp[:].rearrange("p t d -> p (t d)").rearrange("p (k n) -> p k n", k=8)
        xn8 = xn[:].rearrange("p t d -> p (t d)").rearrange("p (k n) -> p k n", k=8)
        conv_out = (xn8, tiles(QA), tiles(KA))
        for g in range(3):
            V.after(Tick(A, evacs - 12 + 4 * (g + 1), None))
            for _ in conv_steps(chip, conv_out[g], tiles(8 * g), 5,
                                lambda k, g=g: chip.vec[:, 8 + 24 * k + 8 * g:8 + 24 * k + 8 * g + 8], scr, lambda k: k - 2):
                pass
        conv = Tick(V, V.n, None)

        def col(n):
            return sf[:, 64 + 32 * n:96 + 32 * n].rearrange("p (t c) -> p t c", t=NT)

        beta, gl, Gc, eG, bG, kdec = (col(n) for n in range(6))
        egl = sf[:, 256:320].rearrange("p (t k c) -> p t k c", t=NT, k=2)
        own = sf[:, 320:352].rearrange("p (t c) -> p t c", t=NT)
        norms = sf[:, 352:384]
        state = {}

        def rates():
            ab = ps[4][:, 0:64].rearrange("p (t c) -> p t c", t=NT)
            A.after(ab_ready)
            V.after(A.done(act.activation(beta, ab[:, :, 0:16], ACT.Sigmoid)))
            yield
            V.link(v.tensor_tensor(own, ab[:, :, 16:32], dt.unsqueeze(1).to_broadcast([P, NT, 16]), ALU.add))
            softplus(chip, gl, own, [chip.sp_tmp[:, j, :].rearrange("p (t c) -> p t c", t=NT) for j in range(3)])
            g_ready = V.link(v.tensor_tensor(gl, gl, nea.unsqueeze(1).to_broadcast([P, NT, 16]), ALU.mult))
            yield
            T.after(g_ready)
            for t in range(NT):
                for d in range(2):
                    ten.matmul(ps[3][:, 16 * t + 8 * d:16 * t + 8 * d + 8], lhsT=const["up_incl" if d == 0 else "low_incl"],
                               rhs=gl[:, t, 8 * d:8 * d + 8], start=True, stop=True)
                ten.matmul(ps[3][:, 32 + 16 * t:48 + 16 * t], lhsT=const["same_chunk"], rhs=gl[:, t, :], start=True, stop=True)
                for c in range(2):
                    m = ten.matmul(ps[3][:, 64 + 32 * t + 16 * c:80 + 32 * t + 16 * c], lhsT=const[f"chunk_{c}"],
                                   rhs=gl[:, t, :], start=True, stop=True)
            m = T.done(m)
            V.after(m)
            V.link(v.tensor_copy(sf[:, 128:160], ps[3][:, 0:32]))
            kd_ = V.link(v.tensor_tensor(sf[:, 224:256], ps[3][:, 32:64], sf[:, 128:160], ALU.subtract))
            A.after(kd_)
            A.done(act.activation(sf[:, 224:256], sf[:, 224:256], ACT.Exp))
            A.done(act.activation(sf[:, 256:320], ps[3][:, 64:128], ACT.Exp))
            e_ = A.done(act.activation(sf[:, 160:192], sf[:, 128:160], ACT.Exp))
            V.after(e_)
            state["rates"] = V.link(v.tensor_tensor(bG, beta, eG, ALU.mult))
            yield

        def block(b, product, empty):
            bank = 6 + b % 2
            chip.weights_wait(b)
            T.after(bank_read[bank])
            for c in range(2):
                m = product(w2[b % RING], ps[bank], c)
                if c:
                    m.then_inc(chip.w_used, 1)
                else:
                    yield
            bank_read[bank] = empty(ps[bank], b)
            yield

        def feature_major(x):
            def product(w, bank, c):
                for k in range(KD):
                    m = ten.matmul(bank[:, c * SEQ:(c + 1) * SEQ], lhsT=w[:, k, c * P:(c + 1) * P], rhs=x[:, k, :],
                                   start=k == 0, stop=k == KD - 1)
                return m
            return product

        def token_major(x):
            def product(w, bank, t):
                for k in range(KD):
                    m = ten.matmul(bank[:, t * BLK2:(t + 1) * BLK2], lhsT=x[:, k, t * P:(t + 1) * P], rhs=w[:, k, :],
                                   start=k == 0, stop=k == KD - 1)
                return m
            return product

        def copy_to(dst):
            def empty(bank, b):
                act.wait_ge(chip.w_used, b + 1)
                return A.done(act.activation(dst, bank[:].rearrange("p (c n) -> p c n", c=2), ACT.Copy))
            return empty

        def project(name, first_tile):
            for q in range(4):
                yield from block(block_of[name] + q, feature_major(xT), copy_to(tiles(first_tile + 2 * q, 2)))

        def projections():
            for q in range(4):
                yield from block(block_of["vb"] + q, token_major(xT), copy_to(vb[:, :, q * BLK2:(q + 1) * BLK2]))
            yield from project("zb", ZB)
            A.after(bank_read[6], bank_read[7])
            state["zb"] = A.done(act.activation(tiles(ZB), tiles(ZB), ACT.Silu))
            for name, a, fn in (("za", ZA, ACT.Silu), ("ga", GA, ACT.Sigmoid), ("gb", GB, ACT.Sigmoid)):
                yield from project(name, a)
                A.after(bank_read[6], bank_read[7])
                state[name] = A.done(act.activation(tiles(a), tiles(a), fn))

        def attention():
            V.after(bank_read[6], bank_read[7])
            T.after(bank_read[6], bank_read[7], state["rates"])
            rot = []
            for j in range(8):
                x2 = tiles(QB + 2 * j, 2)
                bank = ps[4 + j % 2]
                if j >= 2:
                    T.after(rot[j - 2])
                for u in range(2):
                    m = ten.matmul(bank[:, u * SEQ:(u + 1) * SEQ], lhsT=const["rope_turn"], rhs=x2[:, u, :], start=True, stop=True)
                m = T.done(m)
                V.after(m)
                t1 = pflat[:, (j % 4) * 512:(j % 4 + 1) * 512].rearrange("p (a n) -> p a n", a=2)
                V.done(v.tensor_tensor(t1, bank[:].rearrange("p (a n) -> p a n", a=2), sin.unsqueeze(1).to_broadcast([P, 2, SEQ]), ALU.mult))
                V.link(v.tensor_tensor(x2, x2, cos.unsqueeze(1).to_broadcast([P, 2, SEQ]), ALU.mult))
                rot.append(V.link(v.tensor_tensor(x2, x2, t1, ALU.add)))
                if j % 2:
                    yield
            scale = float(DH) ** -0.5
            mx, sm_, rc, cf = st[:, 8:12], st[:, 16:20], st[:, 24:26], st[:, 28:30]
            pbuf = pflat[:, 0:1024].rearrange("p (c n) -> p c n", c=4)
            aT = pflat[:, 1024:1536]
            T.after(rot[-1])
            o_read = None
            b0, b1 = ps[4], ps[5]
            for hd in range(DHEADS):
                T.after(o_read)
                for c in range(2):
                    for t in range(NT):
                        m = ten.matmul((b0, b1)[c][:, t * SEQ:(t + 1) * SEQ], lhsT=z[64 * c:64 * c + 64, QB + hd, t * P:(t + 1) * P],
                                       rhs=z[64 * c:64 * c + 64, KB + hd, :], start=True, stop=True)
                    m = T.done(m)
                V.after(m)
                yield
                for c in range(2):
                    V.done(v.tensor_reduce(mx[:, 2 * c:2 * c + 2], (b0, b1)[c][:].rearrange("p (t n) -> p t n", t=NT), AX, ALU.max))
                V.after(Tick(V, V.n, None))
                A.after(V.link(v.tensor_scalar(mx, mx, -scale, None, ALU.mult)))
                for c in range(2):
                    for t in range(NT):
                        ex = A.done(act.activation(pbuf[:, 2 * c + t, :], (b0, b1)[c][:, t * SEQ:(t + 1) * SEQ], ACT.Exp,
                                                   bias=mx[:, 2 * c + t:2 * c + t + 1], scale=scale,
                                                   accum_out=sm_[:, 2 * c + t:2 * c + t + 1]))
                yield
                V.after(ex)
                V.done(v.reciprocal(rc, sm_[:, 0:2]))
                V.link(v.reciprocal(cf, sm_[:, 2:4]))
                V.link(v.tensor_tensor(cf, cf, sm_[:, 0:2], ALU.mult))
                V.link(v.tensor_scalar(cf, cf, lam, -1.0, ALU.mult, ALU.mult))
                for t in range(NT):
                    df = V.done(v.scalar_tensor_tensor(out=pbuf[:, t, :], in0=pbuf[:, 2 + t, :], scalar=cf[:, t:t + 1],
                                                       in1=pbuf[:, t, :], op0=ALU.mult, op1=ALU.add))
                yield
                T.after(df)
                for kt in range(2):
                    for t in range(NT):
                        m = ten.transpose(b0[:, (kt * 2 + t) * P:(kt * 2 + t + 1) * P], pbuf[:, t, kt * P:(kt + 1) * P], ident)
                A.after(T.done(m))
                yield
                at_ = A.done(act.activation(aT, b0[:], ACT.Copy))
                T.after(at_)
                for t in range(NT):
                    for kt in range(2):
                        m = ten.matmul(b1[:, t * P:(t + 1) * P], lhsT=aT[:, (kt * 2 + t) * P:(kt * 2 + t + 1) * P],
                                       rhs=vb[:, kt, hd * P:(hd + 1) * P], start=kt == 0, stop=kt == 1)
                m = T.done(m)
                yield
                V.after(m)
                for t in range(NT):
                    o_read = V.done(v.tensor_scalar(z[:, QB + hd, t * P:(t + 1) * P], b1[:, t * P:(t + 1) * P],
                                                    rc[:, t:t + 1], None, ALU.mult))
            V.after(o_read)

        def head_norm_gate(o_of, silu_z, gain, dst, sums, sq, banks):
            for t in range(NT):
                o, q3 = o_of(t), sq[:, t * D:(t + 1) * D].rearrange("p (h n) -> p h n", n=P)
                V.link(v.tensor_tensor(q3, o, o, ALU.mult))
                V.link(v.tensor_reduce(sums[:, 8 * t:8 * t + 8], q3, AX, ALU.add))
                yield
            A.after(V.link(v.tensor_scalar(sums, sums, 1.0 / DK, EPS, ALU.mult, ALU.add)))
            V.after(A.done(act.activation(sums, sums, ACT.Sqrt)))
            V.link(v.reciprocal(sums, sums))
            out_ = []
            for t in range(NT):
                o = o_of(t)
                T.after(V.link(v.tensor_tensor(o, o, sums[:, 8 * t:8 * t + 8].unsqueeze(2).to_broadcast([P, 8, P]), ALU.mult)))
                for q in range(2):
                    if len(out_) >= len(banks):
                        T.after(out_[-len(banks)])
                    bank = banks[(2 * t + q) % len(banks)]
                    for j in range(4):
                        m = ten.transpose(bank[:, j * P:(j + 1) * P], o[:, 4 * q + j, :], ident)
                    V.after(T.done(m))
                    out_.append(V.link(v.scalar_tensor_tensor(
                        out=dst[:, 4 * q:4 * q + 4, t * P:(t + 1) * P], in0=bank[:].rearrange("p (j n) -> p j n", j=4),
                        scalar=gain, in1=silu_z[:, 4 * q:4 * q + 4, t * P:(t + 1) * P], op0=ALU.mult, op1=ALU.mult)))
                    yield

        def branch(name, y_t, gate, dst, start_):
            T.after(Tick(V, V.n, None))
            V.after(state["gb"])
            for q in range(4):
                sl = slice(2 * q, 2 * q + 2)

                def empty(bank, b, sl=sl):
                    v.wait_ge(chip.w_used, b + 1)
                    y = bank[:].rearrange("p (c n) -> p c n", c=2)
                    if start_:
                        return V.link(v.tensor_tensor(dst[:, sl, :], gate[:, sl, :], y, ALU.mult))
                    read = V.link(v.tensor_tensor(gate[:, sl, :], gate[:, sl, :], y, ALU.mult))
                    V.link(v.tensor_tensor(dst[:, sl, :], dst[:, sl, :], gate[:, sl, :], ALU.add))
                    return read

                yield from block(block_of[name] + q, feature_major(y_t), empty)

        def side(other):
            yield from attention()
            while "zb" not in state:
                next(other)
                yield
            V.after(state["zb"])
            yield from head_norm_gate(lambda t: z[:, QB:QB + 8, t * P:(t + 1) * P], tiles(ZB), subl, tiles(KB),
                                      st[:, 32:48], pflat, ps[4:6])

        bufs = [[heads(ar[:, (5 * e + n) * 512:(5 * e + n + 1) * 512]) for n in range(5)] for e in range(2)]

        def over(c):
            return c.unsqueeze(1).to_broadcast([P, 4, P])

        def per_row(c):
            return c.unsqueeze(2).to_broadcast([P, 4, P])

        def delta_inputs():
            sq = ar[:, 0:1024].rearrange("p (b n) -> p b n", b=2)
            T.after(qkv_ready)
            free = [None, None, None, state["rates"]]
            n_ = 0
            for src, dst, ssc in ((KA, k_tok, 0), (QA, q_tok, 16), (VA, v_tok, None)):
                for t in range(NT):
                    for q in range(2):
                        T.after(free[n_ % 4])
                        bank = ps[n_ % 4]
                        for j in range(4):
                            m = ten.transpose(bank[:, j * P:(j + 1) * P], z[:, src + 4 * q + j, t * P:(t + 1) * P], ident)
                        A.after(T.done(m))
                        free[n_ % 4] = A.done(act.activation(dst[:, t, q * BLK:(q + 1) * BLK], bank[:], ACT.Copy))
                        if ssc is not None:
                            A.after(Tick(V, V.n, None))
                            free[n_ % 4] = A.done(act.activation(sq[:, n_ % 2, :], bank[:], ACT.Square))
                            V.after(free[n_ % 4])
                            c0 = ssc + 8 * t + 4 * q
                            V.link(v.tensor_reduce(norms[:, c0:c0 + 4], heads(sq[:, n_ % 2, :]), AX, ALU.add))
                        n_ += 1
                        if n_ % 2 == 0:
                            yield
            tok_ready = Tick(A, A.n, None)
            A.after(V.link(v.tensor_scalar(norms, norms, EPS, None, ALU.add)))
            V.after(A.done(act.activation(norms, norms, ACT.Sqrt)))
            V.link(v.reciprocal(norms, norms))
            V.link(v.tensor_scalar(norms[:, 16:32], norms[:, 16:32], float(DK) ** -0.5, None, ALU.mult))
            V.after(tok_ready)
            for buf, c0, back in ((k_tok, 0, KA), (q_tok, 16, QA)):
                for t in range(NT):
                    b3 = heads(buf[:, t, :])
                    T.after(V.link(v.tensor_tensor(b3, b3, per_head(norms[:, c0 + 8 * t:c0 + 8 * t + 8]), ALU.mult)))
                    for q in range(2):
                        T.after(free[n_ % 4])
                        bank = ps[n_ % 4]
                        for j in range(4):
                            m = ten.transpose(bank[:, j * P:(j + 1) * P], buf[:, t, (4 * q + j) * P:(4 * q + j + 1) * P], ident)
                        A.after(T.done(m))
                        free[n_ % 4] = A.done(act.activation(z[:, back + 4 * q:back + 4 * q + 4, t * P:(t + 1) * P],
                                                             heads(bank[:]), ACT.Copy))
                        n_ += 1
                    yield
            T.after(Tick(A, A.n, None))
            V.after(Tick(A, A.n, None), Tick(T, T.n, None))

        def delta_inverses(d):
            dn, up = ("low", "up") if d == 0 else ("up", "low")
            V.after(Tick(T, T.n, None), Tick(A, A.n, None))
            T.after(Tick(A, A.n, None))
            A.after(Tick(V, V.n, None), Tick(T, T.n, None))
            G.after(Tick(V, V.n, None), Tick(T, T.n, None))
            banks_free, bufs_free = [], []
            for hg in range(2):
                dh = slice(8 * d + 4 * hg, 8 * d + 4 * hg + 4)
                T.after(*banks_free)
                A.after(*bufs_free)
                V.after(*bufs_free)
                got, tm, tt, ls = [None] * 2, [None] * 2, [None] * 2, [None] * 2
                for e in range(2):
                    Tm, TT, LT, X, Ls = bufs[e]
                    for j in range(4):
                        kT = z[:, KA + 4 * hg + j, e * P:(e + 1) * P]
                        m = ten.matmul(ps[2 * e][:, j * P:(j + 1) * P], lhsT=kT, rhs=kT, start=True, stop=True)
                    V.after(T.done(m))
                    V.link(v.tensor_tensor(Tm, heads(ps[2 * e][:]), per_row(beta[:, e, dh]), ALU.mult))
                    for j in range(4):
                        c = 8 * d + 4 * hg + j
                        ten.matmul(ps[2 * e + 1][:, j * P:(j + 1) * P], lhsT=ident, rhs=const[dn + "_far"], start=True, stop=False)
                        m = ten.matmul(ps[2 * e + 1][:, j * P:(j + 1) * P], lhsT=gl[:, e, c:c + 1].to_broadcast([P, P]),
                                       rhs=const["up_incl" if d == 0 else "low_incl"], start=False, stop=True)
                    A.after(T.done(m))
                    for j in range(4):
                        c = 8 * d + 4 * hg + j
                        got[e] = A.done(act.activation(X[:, j, :], ps[2 * e + 1][:, j * P:(j + 1) * P], ACT.Exp, scale=-1.0,
                                                       bias=Gc[:, e, c:c + 1]))
                yield
                for e in range(2):
                    Tm, TT, LT, X, Ls = bufs[e]
                    T.after(got[e])
                    V.after(got[e])
                    l_ = V.link(v.tensor_tensor(Tm, X, Tm, ALU.mult))
                    for j in range(4):
                        m = ten.transpose(ps[2 * e + 1][:, j * P:(j + 1) * P], X[:, j, :], ident)
                    A.after(T.done(m))
                    dT = A.done(act.activation(Ls, heads(ps[2 * e + 1][:]), ACT.Copy))
                    T.after(l_)
                    for j in range(4):
                        m = ten.transpose(ps[2 * e][:, j * P:(j + 1) * P], Tm[:, j, :], ident)
                    lt = T.done(m)
                    T.after(dT)
                    for j in range(4):
                        m = ten.matmul(ps[2 * e + 1][:, j * P:(j + 1) * P], lhsT=z[:, KA + 4 * hg + j, e * P:(e + 1) * P],
                                       rhs=z[:, QA + 4 * hg + j, e * P:(e + 1) * P], start=True, stop=True)
                    got[e] = (lt, dT, T.done(m))
                yield
                for e in range(2):
                    Tm, TT, LT, X, Ls = bufs[e]
                    lt, dT, qk = got[e]
                    A.after(lt)
                    lt_ = A.done(act.activation(LT, heads(ps[2 * e][:]), ACT.Copy))
                    V.after(dT, qk)
                    q_ = V.link(v.tensor_tensor(heads(QK[d][:, e, hg * BLK:(hg + 1) * BLK]), Ls, heads(ps[2 * e + 1][:]), ALU.mult))
                    G.after(lt_, q_)
                    ls[e] = G.done(pool.tensor_tensor(Ls, LT, over(const[up + "_2"]), ALU.mult))
                    G.link(pool.tensor_tensor(TT, LT, over(const[up + "_1"]), ALU.mult))
                    tt[e] = G.link(pool.tensor_tensor(TT, over(ident), TT, ALU.subtract))
                    V.after(lt)
                    V.link(v.tensor_tensor(Tm, Tm, over(const[dn + "_1"]), ALU.mult))
                    tm[e] = V.link(v.tensor_tensor(Tm, over(ident), Tm, ALU.subtract))
                for s in (2, 4, 8, 16, 32):
                    last = s == 32
                    for e in range(2):
                        Tm, TT, LT, X, Ls = bufs[e]
                        T.after(ls[e], tm[e], lt_)
                        for j in range(4):
                            m = ten.matmul(ps[2 * e][:, j * P:(j + 1) * P], lhsT=Ls[:, j, :], rhs=Tm[:, j, :], start=True, stop=True)
                        m = T.done(m)
                        A.after(m)
                        got[e] = A.done(act.activation(X, heads(ps[2 * e][:]), ACT.Copy))
                        G.after(m)
                        if not last:
                            ls[e] = G.link(pool.tensor_tensor(Ls, LT, over(const[f"{up}_{2 * s}"]), ALU.mult))
                    yield
                    for e in range(2):
                        Tm, TT, LT, X, Ls = bufs[e]
                        T.after(got[e], tt[e])
                        for j in range(4):
                            if not last:
                                ten.matmul(ps[2 * e][:, j * P:(j + 1) * P], lhsT=TT[:, j, :], rhs=X[:, j, :], start=True, stop=True)
                            m = ten.matmul(ps[2 * e + 1][:, j * P:(j + 1) * P], lhsT=X[:, j, :], rhs=TT[:, j, :], start=True, stop=True)
                        got[e] = T.done(m)
                    yield
                    for e in range(2):
                        Tm, TT, LT, X, Ls = bufs[e]
                        V.after(got[e], tt[e])
                        if not last:
                            tm[e] = V.done(v.tensor_tensor(Tm, Tm, heads(ps[2 * e][:]), ALU.subtract))
                        tt[e] = V.link(v.tensor_tensor(TT, TT, heads(ps[2 * e + 1][:]), ALU.subtract))
                bufs_free, banks_free = [], []
                for e in range(2):
                    Tm, TT, LT, X, Ls = bufs[e]
                    G.after(tt[e])
                    ls[e] = G.link(pool.tensor_tensor(Ls, TT, per_row(bG[:, e, dh]), ALU.mult))
                    T.after(V.link(v.tensor_tensor(X, TT, per_row(beta[:, e, dh]), ALU.mult)))
                    for j in range(4):
                        cs = slice((4 * hg + j) * P, (4 * hg + j + 1) * P)
                        m = ten.matmul(ps[2 * e][:, j * P:(j + 1) * P], lhsT=X[:, j, :], rhs=v_tok[:, e, cs], start=True, stop=True)
                    A.after(T.done(m))
                    A.done(act.activation(U_[d][:, e, hg * BLK:(hg + 1) * BLK], ps[2 * e][:], ACT.Copy))
                    T.after(ls[e])
                    for j in range(4):
                        cs = slice((4 * hg + j) * P, (4 * hg + j + 1) * P)
                        m = ten.matmul(ps[2 * e + 1][:, j * P:(j + 1) * P], lhsT=k_tok[:, e, cs], rhs=Ls[:, j, :], start=True, stop=True)
                    m = T.done(m)
                    bufs_free.append(m)
                    A.after(m)
                    banks_free.append(A.done(act.activation(w_T[d][:, e, hg * BLK:(hg + 1) * BLK], ps[2 * e + 1][:], ACT.Copy)))
                yield

        def delta_state(d):
            bk = ps[4 * d:4 * d + 4]
            u_d, w_d, qk_d = U_[d], w_T[d], QK[d]
            KDb = (v_tok, k_tok)[d]
            S8 = heads(ar[:, d * 1024:(d + 1) * 1024])
            part = ar[:, 2048 + 1024 * d:3072 + 1024 * d]
            for t in range(NT):
                s_tick = V.link(v.tensor_tensor(heads(KDb[:, t, :]), heads(k_tok[:, t, :]), per_head(kdec[:, t, 8 * d:8 * d + 8]), ALU.mult))
            mid_free = None
            for n, c in enumerate(range(4) if d == 0 else range(3, -1, -1)):
                t, lo = c // 2, CHUNK * (c % 2)
                rows_ = slice(lo, lo + CHUNK)
                T.after(s_tick)
                if n:
                    for hh in range(8):
                        m = ten.matmul(bk[hh // 4][rows_, (hh % 4) * P:(hh % 4 + 1) * P],
                                       lhsT=w_d[:, t, hh * P + lo:hh * P + lo + CHUNK], rhs=S8[:, hh, :], start=True, stop=True)
                    m = T.done(m)
                    T.after(mid_free)
                    for hh in range(8):
                        mi = ten.matmul(bk[2 + hh // 4][rows_, (hh % 4) * P:(hh % 4 + 1) * P],
                                        lhsT=z[:, QA + hh, t * P + lo:t * P + lo + CHUNK], rhs=S8[:, hh, :], start=True, stop=True)
                    inter = T.done(mi)
                    yield
                    V.after(m)
                    for q in range(2):
                        cs = slice(q * BLK, (q + 1) * BLK)
                        u_tick = V.link(v.tensor_tensor(u_d[rows_, t, cs], u_d[rows_, t, cs], bk[q][rows_, :], ALU.subtract))
                    T.after(u_tick)
                for hh in range(8 if n < 3 else 0):
                    m = ten.matmul(bk[hh // 4][:, (hh % 4) * P:(hh % 4 + 1) * P], lhsT=KDb[rows_, t, hh * P:(hh + 1) * P],
                                   rhs=u_d[rows_, t, hh * P:(hh + 1) * P], start=True, stop=True)
                if n < 3:
                    m = T.done(m)
                if n:
                    V.after(inter)
                    for q in range(2):
                        cs = slice(q * BLK, (q + 1) * BLK)
                        e3 = eG[rows_, t, 8 * d + 4 * q:8 * d + 4 * q + 4].unsqueeze(2).to_broadcast([CHUNK, 4, P])
                        mid_free = V.link(v.tensor_tensor(heads(part[rows_, cs]), heads(bk[2 + q][rows_, :]), e3, ALU.mult))
                    G.after(mid_free)
                    G.link(pool.tensor_tensor(O[rows_, t, :], O[rows_, t, :], part[rows_, :], ALU.add))
                    if n < 3:
                        G.after(inter)
                        for q in range(2):
                            s4 = S8[:, 4 * q:4 * q + 4, :]
                            scaled = G.link(pool.tensor_tensor(s4, s4, per_row(egl[:, t, c % 2, 8 * d + 4 * q:8 * d + 4 * q + 4]), ALU.mult))
                yield
                V.after(m)
                if n < 3:
                    for q in range(2):
                        s4 = S8[:, 4 * q:4 * q + 4, :]
                        if n == 0:
                            s_tick = V.link(v.tensor_copy(s4, heads(bk[q][:])))
                        else:
                            V.after(scaled)
                            s_tick = V.link(v.tensor_tensor(s4, s4, heads(bk[q][:]), ALU.add))
                if n % 2:
                    T.after(mid_free)
                    for hh in range(8):
                        m = ten.matmul(bk[2 + hh // 4][:, (hh % 4) * P:(hh % 4 + 1) * P], lhsT=qk_d[:, t, hh * P:(hh + 1) * P],
                                       rhs=u_d[:, t, hh * P:(hh + 1) * P], start=True, stop=True)
                    m = T.done(m)
                    yield
                    V.after(m)
                    V.after(Tick(G, G.n, None))
                    for q in range(2):
                        cs = slice(q * BLK, (q + 1) * BLK)
                        mid_free = V.link(v.tensor_tensor(O[:, t, cs], O[:, t, cs], bk[2 + q][:], ALU.add))

        def per_head(c):
            return c.unsqueeze(2).to_broadcast([P, 8, P])

        rate_steps = rates()
        next(rate_steps)
        for _ in project("qb", QB):
            pass
        A.after(conv)
        A.link(act.activation(tiles(VA), tiles(KA), ACT.Silu))
        A.link(act.activation(tiles(KA), tiles(QA), ACT.Silu))
        qkv_ready = A.link(act.activation(tiles(QA), xn8, ACT.Silu))
        proj = chain_of(project("kb", KB), projections())
        other = side(proj)
        next(rate_steps)
        for _ in range(4):
            next(proj)
        next(rate_steps)
        def weave(main, pace):
            for _, steps in zip_longest(main, pace):
                for s in steps or "":
                    next({"p": proj, "a": other}[s], None)

        weave(delta_inputs(), PACE_INPUTS)
        weave(delta_inverses(0), PACE_FIRST)
        for _ in other:
            next(proj, None)
        weave(delta_inverses(1), PACE_SECOND)
        for _ in proj:
            pass
        V.after(Tick(T, T.n, None), Tick(A, A.n, None), zeroed)
        T.after(Tick(A, A.n, None))
        streams = [delta_state(0), delta_state(1)]
        while streams:
            for g in tuple(streams):
                if next(g, streams) is streams:
                    streams.remove(g)
        V.after(state["za"])
        T.after(Tick(V, V.n, None))
        bank_read[6] = bank_read[7] = Tick(V, V.n, None)
        pb = branch("w_pb_2", tiles(KB), tiles(GB), tiles(GB), True)
        for _ in head_norm_gate(lambda t: heads(O[:, t, :]), tiles(ZA), chip.vec[:, 128:129], tiles(QA), st[:, 48:64],
                                ar[:, 0:2048], ps[0:4]):
            next(pb, None)
        for _ in pb:
            pass
        for _ in branch("w_pa_2", tiles(QA), tiles(GA), tiles(GB), False):
            pass
        T.after(Tick(V, V.n, None))
        for q in range(4):
            def add_to_h(bank, b, q=q):
                v.wait_ge(chip.w_used, b + 1)
                hs = h[:, :, q * BLK2:(q + 1) * BLK2]
                return V.done(v.tensor_tensor(hs, hs, bank[:].rearrange("p (t n) -> p t n", t=NT), ALU.add))

            for _ in block(block_of["w_out_2"] + q, token_major(tiles(GB)), add_to_h):
                pass
        chip.reset()


BLOCK1 = ("x", "p", "norm_mix", "w_in", "attn_sinks", "conv_w", "rec_conv_w", "rec_conv_b", "w_rgate", "b_rgate", "w_igate",
          "b_igate", "lru_lambda", "w_branch", "w_out", "norm_ffn", "w_peer_q", "peer_sub_keys", "peer_u", "peer_v",
          "norm_ple", "w_ple_gate", "w_ple_proj", "norm_final")
BLOCK2 = ("positions_2", "norm_w_2", "w_in_2", "conv_w_2", "a_log_2", "dt_bias_2", "gdn_norm_w_2", "diff_lambda_2",
          "diff_subln_w_2", "w_pa_2", "w_pb_2", "w_out_2", "final_norm_w_2")


def build(nc, io, out):
    chip = Chip(nc, io["constants"])
    chip.sp_tmp = chip.sb("softplus_scratch", [P, 3, 32])
    tables = chip.sb("rope_tables", [P, 2, SEQ])
    nc.sync.dma_start(chip.h[:], io["x"][0].rearrange("(t p) d -> p t d", p=P)).then_inc(chip.const_sem, 16)
    for e in (nc.tensor, nc.vector, nc.scalar, nc.gpsimd):
        e.wait_ge(chip.const_sem, 32)
    chip.reset()
    block_one(chip, io)
    final_norm(chip, chip.h, io["norm_final"])
    block_two(chip, io, (tables[:, 0, :], tables[:, 1, :]))
    done = final_norm(chip, chip.xn, io["final_norm_w_2"])
    nc.sync.wait_ge(chip.V.sem, done.n)
    chip.store.start(nc.sync.dma_start(out[0].rearrange("(t p) d -> p t d", p=P), chip.xn[:]))
    nc.sync.wait_ge(chip.store.sem, 16)


def kernel(**inputs):
    import concourse.bacc as bacc
    from concourse.bass_utils import run_bass_kernel_spmd

    nc = bacc.Bacc("TRN2", target_bir_lowering=False, num_devices=1)
    arrays = {n: np.ascontiguousarray(inputs[n]) for n in BLOCK1 + BLOCK2}
    arrays["constants"] = const_array()
    arrays["lambda_init"] = np.array([[0.8 - 0.6 * np.exp(-0.3 * l)] for l in range(DEPTH)], np.float32)
    io = {n: nc.dram_tensor(n, a.shape, mybir.dt.from_np(a.dtype), kind="ExternalInput").ap() for n, a in arrays.items()}
    out = nc.dram_tensor("out", (1, SEQ, D), F32, kind="ExternalOutput").ap()
    build(nc, io, out)
    r = run_bass_kernel_spmd(nc, [arrays], core_ids=[0])
    return r.results[0]["out"]
```
